# Optimizing a Trainium2 kernel written in Bass

```python
import jax, jax.numpy as jnp
from jax import lax
import numpy as np

D_MODEL = 1024
BATCH = 1
SEQ = 256
DEPTH = 2

ATT_HEADS = 8
ATT_KV_HEADS = 2
HEAD_DIM = 64
WINDOW = 128
ATT_BLOCK = 128
ATT_WIDTH = ATT_HEADS * HEAD_DIM
KV_WIDTH = ATT_KV_HEADS * HEAD_DIM
CONV_WIDTH = 512
CONV_K = 3
POOL_SIZES = (2, 4, 8, 16)
POOL_GROUP = 128
POOL_WIDTH = 512
SGU_GROUPS = 4
SGU_CHUNK = 128
SGU_WIDTH = 512
SGU_GROUP = SGU_WIDTH // SGU_GROUPS
N_BRANCH = 4
BRANCH_WIDTH = 512
IN_COLS = ATT_WIDTH + 2 * KV_WIDTH + 3 * CONV_WIDTH + POOL_WIDTH + 2 * SGU_WIDTH + N_BRANCH * D_MODEL
FFN_HIDDEN = 2816
N_EXPERTS = 8
TOP_K = 2
N_DENSE = (DEPTH + 1) // 2
N_MOE = DEPTH // 2
RMS_EPS = 1e-6
NEG_INF = -1e30

kernel_name = "hybrid_gated_multimixer_moe_trunk"

def rmsnorm(x, g):
    xf = x.astype(jnp.float32)
    y = xf * lax.rsqrt(jnp.mean(xf * xf, axis=-1, keepdims=True) + RMS_EPS)
    return (y * g.astype(jnp.float32)).astype(x.dtype)

def sliding_window_attention(q, k, v, sinks):
    b, s, _ = q.shape
    nb = s // ATT_BLOCK
    grp = ATT_HEADS // ATT_KV_HEADS
    qb = q.reshape(b, nb, ATT_BLOCK, ATT_KV_HEADS, grp, HEAD_DIM)

    def band(t):
        t = t.reshape(b, nb, ATT_BLOCK, ATT_KV_HEADS, HEAD_DIM)
        prev = jnp.pad(t, ((0, 0), (1, 0), (0, 0), (0, 0), (0, 0)))[:, :-1]
        return jnp.concatenate([prev, t], axis=2)

    kb, vb = band(k), band(v)
    scores = jnp.einsum('bnqkgd,bnskd->bnkgqs', qb, kb).astype(jnp.float32) * (HEAD_DIM ** -0.5)
    qi = jnp.arange(ATT_BLOCK)[:, None]
    kj = jnp.arange(2 * ATT_BLOCK)[None, :]
    rel = qi + ATT_BLOCK - kj
    local = (rel >= 0) & (rel < WINDOW)
    kpos = jnp.arange(nb)[:, None] * ATT_BLOCK - ATT_BLOCK + kj
    valid = local[None] & (kpos >= 0)[:, None, :]
    scores = jnp.where(valid[None, :, None, None], scores, NEG_INF)
    sink_col = jnp.broadcast_to(
        sinks.astype(jnp.float32).reshape(1, 1, ATT_KV_HEADS, grp, 1, 1), scores.shape[:-1] + (1,))
    probs = jax.nn.softmax(jnp.concatenate([scores, sink_col], axis=-1), axis=-1)[..., :-1]
    out = jnp.einsum('bnkgqs,bnskd->bnqkgd', probs.astype(v.dtype), vb)
    return out.reshape(b, s, ATT_WIDTH)

def short_conv_mixer(bgate, cgate, xin, conv_w):
    z = cgate * xin
    s = z.shape[1]
    zp = jnp.pad(z, ((0, 0), (CONV_K - 1, 0), (0, 0)))
    y = sum(conv_w[j] * zp[:, j:j + s] for j in range(CONV_K))
    return bgate * y

def multiscale_pool_mixer(p, pool_w, pool_scale):
    b, s, _ = p.shape
    pf = p.astype(jnp.float32)
    cs = jnp.pad(jnp.cumsum(pf, axis=1), ((0, 0), (1, 0), (0, 0)))
    t = jnp.arange(s)
    outs = []
    for g, w in enumerate(POOL_SIZES):
        sl = slice(g * POOL_GROUP, (g + 1) * POOL_GROUP)
        start = jnp.maximum(t + 1 - w, 0)
        cnt = (t + 1 - start).astype(jnp.float32)
        win_sum = cs[:, 1:, sl] - cs[:, start, sl]
        outs.append(win_sum / cnt[None, :, None] - pf[..., sl])
    pooled = jnp.stack(outs, axis=2).astype(p.dtype)
    y = jnp.einsum('bsgc,gcd->bsgd', pooled, pool_w).reshape(b, s, POOL_WIDTH)
    return y * pool_scale

def spatial_gating_mixer(u, v, sgu_w, sgu_b):
    b, s, _ = u.shape
    nc = s // SGU_CHUNK
    mask = jnp.tril(jnp.ones((SGU_CHUNK, SGU_CHUNK), dtype=bool))
    ws = jnp.where(mask[None], sgu_w, jnp.zeros_like(sgu_w))
    vc = v.reshape(b, nc, SGU_CHUNK, SGU_GROUPS, SGU_GROUP)
    mixed = jnp.einsum('gts,bnsgc->bntgc', ws, vc) + sgu_b.T[None, None, :, :, None]
    return u * mixed.reshape(b, s, SGU_WIDTH)

def hybrid_mixer(h, w_in, sinks, conv_w, pool_w, pool_scale, sgu_w, sgu_b, w_branch, w_out):
    b, s, _ = h.shape
    proj = h @ w_in
    sizes = [ATT_WIDTH, KV_WIDTH, KV_WIDTH, CONV_WIDTH, CONV_WIDTH, CONV_WIDTH,
             POOL_WIDTH, SGU_WIDTH, SGU_WIDTH, N_BRANCH * D_MODEL]
    splits = [int(c) for c in np.cumsum(sizes)[:-1]]
    q, k, v, cb, cc, cx, p, u, sv, g = jnp.split(proj, splits, axis=-1)
    y_att = sliding_window_attention(q, k, v, sinks)
    y_conv = short_conv_mixer(cb, cc, cx, conv_w)
    y_pool = multiscale_pool_mixer(p, pool_w, pool_scale)
    y_sgu = spatial_gating_mixer(u, sv, sgu_w, sgu_b)
    branches = jnp.stack([y_att, y_conv, y_pool, y_sgu], axis=2)
    up = jnp.einsum('bsnc,ncd->bsnd', branches, w_branch)
    gates = jax.nn.sigmoid(g.reshape(b, s, N_BRANCH, D_MODEL))
    merged = jnp.sum(gates * up, axis=2)
    return merged @ w_out

def swiglu(h, w_gate, w_up, w_down):
    return (jax.nn.silu(h @ w_gate) * (h @ w_up)) @ w_down

def moe_swiglu(h, router_w, router_b, w_gate, w_up, w_down):
    logits = (h @ router_w).astype(jnp.float32) + router_b.astype(jnp.float32)
    top_val, top_idx = lax.top_k(logits, TOP_K)
    top_w = jax.nn.softmax(top_val, axis=-1)
    combine = jnp.sum(jax.nn.one_hot(top_idx, N_EXPERTS, dtype=jnp.float32) * top_w[..., None], axis=-2)
    y = jnp.zeros_like(h)
    for e in range(N_EXPERTS):
        y = y + combine[..., e:e + 1].astype(h.dtype) * swiglu(h, w_gate[e], w_up[e], w_down[e])
    return y

def setup_inputs(seed: int = 0) -> dict:
    key = jax.random.key(seed)
    ks = jax.random.split(key, 24)
    nrm = lambda k, shape, scale: jax.random.normal(k, shape, jnp.float32) * scale
    gain = lambda k, shape: 1.0 + 0.05 * jax.random.normal(k, shape, jnp.float32)
    return {
        "x": nrm(ks[0], (BATCH, SEQ, D_MODEL), 1.0),
        "ln_mix_g": gain(ks[1], (DEPTH, D_MODEL)),
        "w_in": nrm(ks[2], (DEPTH, D_MODEL, IN_COLS), D_MODEL ** -0.5),
        "attn_sinks": nrm(ks[3], (DEPTH, ATT_HEADS), 1.0),
        "conv_w": nrm(ks[4], (DEPTH, CONV_K, CONV_WIDTH), CONV_K ** -0.5),
        "pool_w": nrm(ks[5], (DEPTH, len(POOL_SIZES), POOL_GROUP, POOL_GROUP), POOL_GROUP ** -0.5),
        "pool_scale": gain(ks[6], (DEPTH, POOL_WIDTH)),
        "sgu_w": nrm(ks[7], (DEPTH, SGU_GROUPS, SGU_CHUNK, SGU_CHUNK), SGU_CHUNK ** -0.5),
        "sgu_b": gain(ks[8], (DEPTH, SGU_GROUPS, SGU_CHUNK)),
        "w_branch": nrm(ks[9], (DEPTH, N_BRANCH, BRANCH_WIDTH, D_MODEL), BRANCH_WIDTH ** -0.5),
        "w_out": nrm(ks[10], (DEPTH, D_MODEL, D_MODEL), D_MODEL ** -0.5),
        "ln_ffn_g": gain(ks[11], (DEPTH, D_MODEL)),
        "dense_w_gate": nrm(ks[12], (N_DENSE, D_MODEL, FFN_HIDDEN), D_MODEL ** -0.5),
        "dense_w_up": nrm(ks[13], (N_DENSE, D_MODEL, FFN_HIDDEN), D_MODEL ** -0.5),
        "dense_w_down": nrm(ks[14], (N_DENSE, FFN_HIDDEN, D_MODEL), FFN_HIDDEN ** -0.5),
        "router_w": nrm(ks[15], (N_MOE, D_MODEL, N_EXPERTS), D_MODEL ** -0.5),
        "router_b": nrm(ks[16], (N_MOE, N_EXPERTS), 0.01),
        "moe_w_gate": nrm(ks[17], (N_MOE, N_EXPERTS, D_MODEL, FFN_HIDDEN), D_MODEL ** -0.5),
        "moe_w_up": nrm(ks[18], (N_MOE, N_EXPERTS, D_MODEL, FFN_HIDDEN), D_MODEL ** -0.5),
        "moe_w_down": nrm(ks[19], (N_MOE, N_EXPERTS, FFN_HIDDEN, D_MODEL), FFN_HIDDEN ** -0.5),
        "ln_final_g": gain(ks[20], (D_MODEL,)),
    }

def reference(x, ln_mix_g, w_in, attn_sinks, conv_w, pool_w, pool_scale, sgu_w, sgu_b, w_branch, w_out,
              ln_ffn_g, dense_w_gate, dense_w_up, dense_w_down, router_w, router_b,
              moe_w_gate, moe_w_up, moe_w_down, ln_final_g):
    for layer in range(DEPTH):
        h = rmsnorm(x, ln_mix_g[layer])
        x = x + hybrid_mixer(h, w_in[layer], attn_sinks[layer], conv_w[layer], pool_w[layer],
                             pool_scale[layer], sgu_w[layer], sgu_b[layer], w_branch[layer], w_out[layer])
        h = rmsnorm(x, ln_ffn_g[layer])
        i = layer // 2
        if layer % 2 == 0:
            x = x + swiglu(h, dense_w_gate[i], dense_w_up[i], dense_w_down[i])
        else:
            x = x + moe_swiglu(h, router_w[i], router_b[i], moe_w_gate[i], moe_w_up[i], moe_w_down[i])
    return rmsnorm(x, ln_final_g)


_drawn_inputs = setup_inputs


def setup_inputs(seed=0):
    import zlib

    import numpy as np

    out = dict(_drawn_inputs(seed))
    spreads = {}
    factors = {'attn_sinks': 2.871, 'router_b': 6.418}
    for name, (base, spread) in spreads.items():
        noise = np.random.default_rng([zlib.crc32(name.encode()), seed]).standard_normal(out[name].shape)
        drawn = base * np.exp(spread * noise) if base else spread * noise
        out[name] = __import__('jax').numpy.asarray(drawn.astype(out[name].dtype))
    for name, factor in factors.items():
        out[name] = (out[name] * factor).astype(out[name].dtype)
    return out
```

```python
from contextlib import ExitStack

import concourse.bass as bass
from concourse import mybir

P = 128
D = 1024
T = 256
TB = T // P
DC = D // P
LAYERS = 2
HEADS = 8
HD = 64
BRANCHES = 4
CT = 4
FFN = 2816
EXPERTS = 8
EPS = 1e-6
NEG = -1e30

UNIT = 2048
SPLIT_SLOTS = 3
RAW1 = 6
RAW2 = 11
PROJ_UNITS = 15
GATE_UNITS = 3 * 2 * BRANCHES
OUT_UNITS = 4
MIX_UNITS = PROJ_UNITS + GATE_UNITS + OUT_UNITS
SLABS = FFN // 256
DENSE_UNITS = 3 * SLABS
UNITS1 = 2 * MIX_UNITS + DENSE_UNITS
MOE_UNITS = DENSE_UNITS * EXPERTS
EXPERT_UNITS = DENSE_UNITS

F32 = mybir.dt.float32
F32R = mybir.dt.float32r
I32 = mybir.dt.int32
ALU = mybir.AluOpType
ACT = mybir.ActivationFunctionType
AX = mybir.AxisListType

V_MIX_G, V_FFN_G = 0, 16
V_CONV, V_POOL, V_SINK = 32, 56, 64
V_RB = 80
V_RW = 88
V_FIX = 88 + 64
V_MASK = V_FIX + 64
V_IDENT = V_MASK + 256
V_COLS = V_IDENT + 128

ACT_EVACS = 24
DVE_EVACS = 6
X_BEFORE = 4 * (LAYERS + 1)
TURNS_BEFORE = DC * (LAYERS + 1)
BRANCH_ORDER = [0, 1, 3, 2]


def mixer_base(layer):
    return layer * (MIX_UNITS + DENSE_UNITS)


def at(n, more):
    return n + more[0] * more[1] if more else n


def loads(more, ring):
    return more[0] // ring * 16 * more[1] if more else 0


def trunk(nc, x, small, tables, layer_weights, gains, stream1, stream2, out):
    ctx = ExitStack()
    with ctx:
        def sb(name, shape, dt=F32):
            return ctx.enter_context(nc.sbuf_tensor(name, shape, dt))

        def sem(name):
            return ctx.enter_context(nc.semaphore(name))

        raw = sb("raw", [P, RAW2, UNIT])
        w_hi = sb("w_hi", [P, SPLIT_SLOTS, UNIT], F32R)
        w_lo = sb("w_lo", [P, SPLIT_SLOTS, UNIT], F32R)
        xs = sb("xs", [P, TB, D])
        h_hi = sb("h_hi", [P, DC, T], F32R)
        h_lo = sb("h_lo", [P, DC, T], F32R)
        merged = sb("merged", [P, DC, T])
        gate_buf = sb("gate_buf", [P, 2, 512])
        pair_hi = [sb(f"pair{i}_hi", [P, CT * T], F32R) for i in range(2)]
        pair_lo = [sb(f"pair{i}_lo", [P, CT * T], F32R) for i in range(2)]
        act_hi = sb("act_hi", [P, 2 * P], F32R)
        act_lo = sb("act_lo", [P, 2 * P], F32R)
        onehot = sb("onehot", [P, TB, P], F32R)
        onehot_t = sb("onehot_t", [P, TB * P], F32R)
        ident_r = sb("ident_r", [P, P], F32R)
        weights_small = sb("weights_small", [P, 1536])
        vec = sb("vec", [P, V_COLS])
        stat = sb("stat", [P, 128])
        route = sb("route", [P, 320])
        combine_r = sb("combine_r", [P, TB, 16, 2], F32R)
        n_pass_i = sb("n_pass_i", [P, 1], I32)

        bank = [ctx.enter_context(nc.psum_tensor(f"bank{i}", [P, 512], F32)) for i in range(8)]

        scratch = raw[:, RAW1:RAW2, :].rearrange("p s u -> p (s u)")
        t1, t2, t3 = (scratch[:, i * 1024:(i + 1) * 1024] for i in range(3))
        probs = scratch[:, 3072:5120].rearrange("p (h k) -> p h k", h=HEADS)
        probs_t = scratch[:, 5120:6144]
        pool_a = scratch[:, 6144:7168].rearrange("p (g t) -> p g t", g=CT)
        pool_b = scratch[:, 7168:8192].rearrange("p (g t) -> p g t", g=CT)
        qkv_s = scratch[:, 8192:9984]
        q_t = qkv_s[:, 0:1024].rearrange("p (j t) -> p j t", j=4)
        k_t = qkv_s[:, 1024:1280]
        v_t = qkv_s[:, 1280:1536]
        v_nat = qkv_s[:, 1536:1792].rearrange("p (b d) -> p b d", b=TB)
        merged_flat = merged[:, :, :].rearrange("p k t -> p (k t)")
        xn = merged_flat.rearrange("p (b d) -> p b d", b=TB)
        h_hi_flat = h_hi[:, :, :].rearrange("p k t -> p (k t)")
        h_lo_flat = h_lo[:, :, :].rearrange("p k t -> p (k t)")
        gate_flat = gate_buf[:, :, :].rearrange("p q c -> p (q c)")
        sgu_wt = weights_small[:, 0:512].rearrange("p (g t) -> p g t", g=4)
        pool_w = weights_small[:, 512:1024].rearrange("p (g t) -> p g t", g=4)
        sgu_bias = weights_small[:, 1024:1536].rearrange("p (g t) -> p g t", g=4)
        gain_row = weights_small[:, 0:1024]
        iota = weights_small[:, 1024:1152]
        earlier = weights_small[:, 1152:1280]
        ones = weights_small[:, 1280:1408]
        rank8 = weights_small[:, 1408:1416]
        ident = vec[:, V_IDENT:V_IDENT + P]
        mask = vec[:, V_MASK:V_MASK + 256]

        x_loaded = sem("x_loaded")
        vec_loaded = sem("vec_loaded")
        small_loaded = sem("small_loaded")
        tables_loaded = sem("tables_loaded")
        gain_loaded = sem("gain_loaded")
        final_gain_loaded = sem("final_gain_loaded")
        sgu_masked = sem("sgu_masked")
        landed1 = [sem(f"landed1_{i}") for i in range(RAW1)]
        landed2 = [sem(f"landed2_{i}") for i in range(RAW2)]
        hi_ready = sem("hi_ready")
        lo_ready = sem("lo_ready")
        unit_used = sem("unit_used")
        squares_ready = sem("squares_ready")
        variance_ready = sem("variance_ready")
        root_ready = sem("root_ready")
        rstd_ready = sem("rstd_ready")
        xn0_ready = sem("xn0_ready")
        xn1_ready = sem("xn1_ready")
        h_turned = sem("h_turned")
        h_hi_ready = sem("h_hi_ready")
        h_lo_ready = sem("h_lo_ready")
        act_evac = sem("act_evac")
        dve_evac = sem("dve_evac")
        v_turned = sem("v_turned")
        v_ready = sem("v_ready")
        scores_done = sem("scores_done")
        neg_max_ready = sem("neg_max_ready")
        exps_ready = sem("exps_ready")
        probs_ready = sem("probs_ready")
        probs_turned = sem("probs_turned")
        probs_t_ready = sem("probs_t_ready")
        att_done = sem("att_done")
        att_half_done = sem("att_half_done")
        att_hi_ready = sem("att_hi_ready")
        att_lo_ready = sem("att_lo_ready")
        pool_scaled = sem("pool_scaled")
        branch_hi_ready = sem("branch_hi_ready")
        branch_lo_ready = sem("branch_lo_ready")
        mixed_done = sem("mixed_done")
        mixed_ready = sem("mixed_ready")
        pooled_ready = sem("pooled_ready")
        pool_done = sem("pool_done")
        gate_used = sem("gate_used")
        merged_hi_ready = sem("merged_hi_ready")
        merged_lo_ready = sem("merged_lo_ready")
        x_updated = sem("x_updated")
        silu_ready = sem("silu_ready")
        act_ready = sem("act_ready")
        act_hi_ready = sem("act_hi_ready")
        act_lo_ready = sem("act_lo_ready")
        r_turned = sem("r_turned")
        r_copied = sem("r_copied")
        logits_done = sem("logits_done")
        gap_ready = sem("gap_ready")
        exp_gap_ready = sem("exp_gap_ready")
        ident_ready = sem("ident_ready")
        places_done = sem("places_done")
        route_ready = sem("route_ready")
        moe_h_ready = sem("moe_h_ready")
        moe_h_hi_ready = sem("moe_h_hi_ready")
        moe_h_lo_ready = sem("moe_h_lo_ready")
        onehot_ready = sem("onehot_ready")
        gathered = sem("gathered")
        next_hi_ready = sem("next_hi_ready")
        next_lo_ready = sem("next_lo_ready")
        slots_hi_ready = sem("slots_hi_ready")
        slots_lo_ready = sem("slots_lo_ready")
        onehot_turned = sem("onehot_turned")
        onehot_t_ready = sem("onehot_t_ready")
        share_ready = sem("share_ready")
        y_weighted = sem("y_weighted")
        y_hi_ready = sem("y_hi_ready")
        y_lo_ready = sem("y_lo_ready")
        scattered = sem("scattered")
        out_scaled = sem("out_scaled")
        out_stored = sem("out_stored")
        dve_step = sem("dve_step")


        def raw_of(s):
            return raw[:, s % RAW1 if s < UNITS1 else (s - UNITS1) % RAW2, :]

        def split_hi(act, s, more=0):
            if s < UNITS1:
                act.wait_ge(landed1[s % RAW1], 16 * (s // RAW1 + 1) + loads(more, RAW1))
            else:
                act.wait_ge(landed2[(s - UNITS1) % RAW2], 16 * ((s - UNITS1) // RAW2 + 1) + loads(more, RAW2))
            if s >= SPLIT_SLOTS:
                act.wait_ge(unit_used, at(s - SPLIT_SLOTS + 1, more))
            nc.scalar.activation(w_hi[:, s % SPLIT_SLOTS, :], raw_of(s), ACT.Copy).then_inc(hi_ready, 1)

        def split_lo(dve, s, more=0):
            dve.wait_ge(hi_ready, at(s + 1, more))
            if s >= SPLIT_SLOTS:
                dve.wait_ge(unit_used, at(s - SPLIT_SLOTS + 1, more))
            nc.vector.tensor_tensor(w_lo[:, s % SPLIT_SLOTS, :], raw_of(s),
                                    w_hi[:, s % SPLIT_SLOTS, :].bitcast(F32), ALU.subtract).then_inc(lo_ready, 1)

        def moe_unit(i, k):
            return UNITS1 + 2 + 3 * (i - 1) + k if i else UNITS1 + k

        def slab_bank(i):
            return bank[5 if i % SLABS == 0 else i % 2]

        block = ctx.enter_context(nc.Block())

        @block.sync
        def _(sp):
            for s in range(RAW1):
                sp.dma_start(raw[:, s, :], stream1[s]).then_inc(landed1[s], 16)
            rounds = UNITS1 // RAW1
            with sp.Fori(1, rounds) as i:
                for s in range(RAW1):
                    sp.wait_ge(lo_ready, (i - 1) * RAW1 + (s + 1))
                    sp.dma_start(raw[:, s, :], stream1[i * RAW1 + s]).then_inc(landed1[s], 16)
            for n in range(rounds * RAW1, UNITS1):
                sp.wait_ge(lo_ready, n - RAW1 + 1)
                sp.dma_start(raw[:, n % RAW1, :], stream1[n]).then_inc(landed1[n % RAW1], 16)
            for m in range(RAW2):
                if m < RAW1:
                    sp.wait_ge(lo_ready, max(n for n in range(UNITS1) if n % RAW1 == m) + 1)
                elif m == RAW1:
                    sp.wait_ge(branch_lo_ready, 3 * LAYERS)
                sp.dma_start(raw[:, m, :], stream2[m]).then_inc(landed2[m], 16)
            rounds = MOE_UNITS // RAW2
            with sp.Fori(1, rounds) as i:
                for s in range(RAW2):
                    sp.wait_ge(lo_ready, (i - 1) * RAW2 + (UNITS1 + s + 1))
                    sp.dma_start(raw[:, s, :], stream2[i * RAW2 + s]).then_inc(landed2[s], 16)
            sp.wait_ge(route_ready, 1)
            n_pass = sp.value_load(n_pass_i[0:1, 0:1], min_val=1, max_val=2)
            with sp.If(n_pass > 1):
                with sp.Fori(rounds, 2 * rounds) as i:
                    for s in range(RAW2):
                        sp.wait_ge(lo_ready, (i - 1) * RAW2 + (UNITS1 + s + 1))
                        sp.dma_start(raw[:, s, :], stream2[i * RAW2 + (s - MOE_UNITS)]).then_inc(landed2[s], 16)

        @block.gpsimd
        def _(pool):
            pool.dma_start(weights_small[:, :], layer_weights[0]).then_inc(small_loaded, 16)
            for layer in range(LAYERS):
                if layer:
                    pool.wait_ge(pool_done, layer)
                    pool.wait_ge(mixed_ready, layer)
                    pool.dma_start(weights_small[:, :], layer_weights[layer]).then_inc(small_loaded, 16)
                pool.wait_ge(small_loaded, 16 * (layer + 1))
                nc.gpsimd.affine_select(out=sgu_wt, in_=sgu_wt, compare_op=ALU.is_ge, fill=0.0, base=0,
                                        pattern=[[0, 4], [1, P]], channel_multiplier=-1).then_inc(sgu_masked, 1)
            pool.wait_ge(pool_done, LAYERS)
            pool.wait_ge(mixed_ready, LAYERS)
            pool.dma_start(weights_small[:, 1024:1536], tables).then_inc(tables_loaded, 16)
            pool.dma_start(gain_row, gains[0]).then_inc(gain_loaded, 16)
            pool.wait_ge(logits_done, 2)
            pool.dma_start(gain_row, gains[1]).then_inc(final_gain_loaded, 16)

        @block.scalar
        def _(act):
            act.dma_start(xs[:, :, :], x).then_inc(x_loaded, 16)
            act.dma_start(vec[:, :], small).then_inc(vec_loaded, 16)

            def copy(dst, src, scale=1.0):
                return nc.scalar.activation(dst, src, ACT.Copy, scale=scale)

            def ahead(s, more=0):
                split_hi(act, s + 2, more)

            def norm(i):
                if i == 0:
                    act.wait_ge(x_loaded, 16)
                    act.wait_ge(vec_loaded, 16)
                elif i < 4:
                    act.wait_ge(x_updated, 4 * i)
                for b in range(TB):
                    last = nc.scalar.activation(xn[:, b, :], xs[:, b, :], ACT.Square, accum_out=stat[:, b:b + 1])
                last.then_inc(squares_ready, 1)
                act.wait_ge(variance_ready, i + 1)
                nc.scalar.activation(stat[:, 4:6], stat[:, 2:4], ACT.Sqrt).then_inc(root_ready, 1)
                if i < 4:
                    act.wait_ge(rstd_ready, i + 1)
                    copy(xn[:, 0, :], xs[:, 0, :], stat[:, 12:13]).then_inc(xn0_ready, 1)

            def turned_hi(i, gain):
                for k in range(DC):
                    act.wait_ge(h_turned, DC * i + k + 1)
                    copy(h_hi[:, k, :], bank[k][:, 0:T],
                         vec[:, gain + k:gain + k + 1]).then_inc(h_hi_ready, 1)

            def mixer(layer):
                u0 = mixer_base(layer)

                def evac(u, dst, src):
                    act.wait_ge(unit_used, u0 + u + 1)
                    copy(dst, src).then_inc(act_evac, 1)

                def exps(b):
                    keys = P * (b + 1)
                    act.wait_ge(neg_max_ready, TB * layer + b + 1)
                    for h in range(HEADS):
                        nc.scalar.activation(probs[:, h, 0:keys], probs[:, h, 0:keys], ACT.Exp,
                                             bias=stat[:, 24 + h:25 + h], accum_out=stat[:, 32 + h:33 + h])
                    nc.scalar.activation(stat[:, 48:56], stat[:, 40:48], ACT.Exp).then_inc(exps_ready, 1)

                def turned_probs(part):
                    act.wait_ge(probs_turned, 3 * layer + part + 1)
                    if part == 1:
                        act.wait_ge(att_done, TB * layer + 1)
                    if part == 2:
                        act.wait_ge(att_half_done, layer + 1)
                    for q in range(2):
                        last = copy(probs_t[:, q * 512:(q + 1) * 512], bank[5 + q][:, :])
                    last.then_inc(probs_t_ready, 1)

                def attention_hi(b):
                    act.wait_ge(att_done, TB * layer + b + 1)
                    copy(pair_hi[0][:, :].rearrange("p (j t) -> p j t", j=4)[:, :, b * P:(b + 1) * P],
                         bank[4][:, :].rearrange("p (j t) -> p j t", j=4)).then_inc(att_hi_ready, 1)

                def branch_hi(turn, src):
                    if turn == 3:
                        act.wait_ge(pool_scaled, layer + 1)
                    else:
                        act.wait_ge(dve_evac, DVE_EVACS * layer + (4 if turn == 1 else 6))
                    if turn >= 2:
                        act.wait_ge(unit_used, u0 + PROJ_UNITS + 6 * (turn - 1))
                    copy(pair_hi[turn % 2][:, :], src).then_inc(branch_hi_ready, 1)

                norm(2 * layer)
                turned_hi(2 * layer, V_MIX_G + DC * layer)
                ahead(u0 + 0)
                ahead(u0 + 1)
                evac(0, qkv_s[:, 0:512], bank[0][:, :])
                ahead(u0 + 2)
                evac(1, qkv_s[:, 512:1024], bank[1][:, :])
                ahead(u0 + 3)
                evac(2, qkv_s[:, 1024:1536], bank[2][:, :])
                ahead(u0 + 4)
                act.wait_ge(v_turned, layer + 1)
                copy(v_nat, bank[3][:, 0:T].rearrange("p (b d) -> p b d", b=TB)).then_inc(v_ready, 1)
                evac(3, t1[:, 0:512], bank[0][:, :])
                ahead(u0 + 5)
                evac(4, t1[:, 512:1024], bank[1][:, :])
                exps(0)
                ahead(u0 + 6)
                ahead(u0 + 7)
                turned_probs(0)
                ahead(u0 + 8)
                attention_hi(0)
                ahead(u0 + 9)
                exps(1)
                branch_hi(1, t1)
                ahead(u0 + 10)
                ahead(u0 + 11)
                for b in range(TB):
                    last = copy(t3[:, b * 512:(b + 1) * 512], bank[b][:, :])
                last.then_inc(act_evac, 1)
                turned_probs(1)
                ahead(u0 + 12)
                ahead(u0 + 13)
                turned_probs(2)
                ahead(u0 + 14)
                act.wait_ge(dve_evac, DVE_EVACS * (layer + 1))
                evac(13, t1[:, 0:512], bank[1][:, :])
                evac(14, t1[:, 512:1024], bank[2][:, :])
                attention_hi(1)
                for turn in range(BRANCHES):
                    for half in range(2):
                        u = PROJ_UNITS + 6 * turn + 3 * half
                        for q in range(2):
                            ahead(u0 + u + q)
                            act.wait_ge(unit_used, u0 + u + q + 1)
                            n = 16 * layer + 4 * turn + 2 * half + q
                            if n >= 2:
                                act.wait_ge(gate_used, n - 1)
                            nc.scalar.activation(gate_buf[:, q, :], bank[2 * half + q][:, :],
                                                 ACT.Sigmoid).then_inc(act_evac, 1)
                        if turn == BRANCHES - 1 and half == 1:
                            act.wait_ge(gate_used, 16 * layer + 14)
                            copy(h_hi_flat[:, 0:1024], merged_flat[:, 0:1024]).then_inc(merged_hi_ready, 1)
                        ahead(u0 + u + 2)
                        if turn == 1 and half == 0:
                            branch_hi(2, t3)
                        if turn == 2 and half == 0:
                            branch_hi(3, t2)
                act.wait_ge(gate_used, 16 * layer + 16)
                copy(h_hi_flat[:, 1024:2048], merged_flat[:, 1024:2048]).then_inc(merged_hi_ready, 1)
                for u in range(MIX_UNITS - OUT_UNITS, MIX_UNITS):
                    if u0 + u + 2 < UNITS1:
                        ahead(u0 + u)

            def dense():
                base = MIX_UNITS
                norm(1)
                turned_hi(1, V_FFN_G)
                ahead(base)
                ahead(base + 1)
                act.wait_ge(unit_used, base + 1)
                nc.scalar.activation(gate_buf[:, 0, :], bank[0][:, :], ACT.Silu).then_inc(silu_ready, 1)
                with act.Fori(0, (SLABS - 1) // 2) as it:
                    for j in range(2):
                        i = 1 + j
                        s = base + 2 + 3 * j
                        more = (6, it)
                        ahead(s, more)
                        act.wait_ge(act_ready, 2 * it + i)
                        copy(pair_hi[j][:, 0:512], gate_buf[:, j, :]).then_inc(act_hi_ready, 1)
                        ahead(s + 1, more)
                        act.wait_ge(unit_used, 6 * it + (s + 1))
                        nc.scalar.activation(gate_buf[:, i % 2, :], bank[i % 2][:, :],
                                             ACT.Silu).then_inc(silu_ready, 1)
                        ahead(s + 2, more)
                act.wait_ge(act_ready, SLABS)
                copy(pair_hi[0][:, 0:512], gate_buf[:, 0, :]).then_inc(act_hi_ready, 1)
                ahead(base + DENSE_UNITS - 1)

            split_hi(act, 0)
            split_hi(act, 1)
            mixer(0)
            dense()
            mixer(1)

            norm(3)
            for b in range(TB):
                act.wait_ge(moe_h_ready, b + 1)
                copy(h_hi_flat[:, b * D:(b + 1) * D], xn[:, b, :]).then_inc(moe_h_hi_ready, 1)
            act.wait_ge(gap_ready, 1)
            nc.scalar.activation(route[:, 88:90], route[:, 86:88], ACT.Exp).then_inc(exp_gap_ready, 1)

            def silu(i, g):
                act.wait_ge(unit_used, EXPERT_UNITS * g + (moe_unit(i, 1) + 1))
                act.wait_ge(h_turned, TURNS_BEFORE + SLABS * g + i)
                nc.scalar.activation(gate_flat[:, 0:256], slab_bank(i)[:, 0:256], ACT.Silu).then_inc(silu_ready, 1)

            def gathered_hi(g, y=None):
                act.wait_ge(gathered, g + 1)
                if y is not None:
                    act.wait_ge(x_updated, X_BEFORE + 4 * y + 4)
                for q in range(2):
                    last = copy(pair_hi[1][:, q * 512:(q + 1) * 512], bank[5 + q][:, :])
                last.then_inc(next_hi_ready, 1)

            def take_slots(g, used):
                act.wait_ge(unit_used, used)
                act.wait_ge(next_hi_ready, g + 1)
                copy(pair_hi[0][:, :], pair_hi[1][:, :].bitcast(F32)).then_inc(slots_hi_ready, 1)

            def weigh_y(g, used, taken):
                act.wait_ge(unit_used, used)
                act.wait_ge(share_ready, g + 1)
                act.wait_ge(x_updated, X_BEFORE + 4 * g)
                for q in range(2):
                    last = copy(merged_flat[:, q * 512:(q + 1) * 512], bank[3 + q][:, :], stat[:, 60:61])
                last.then_inc(y_weighted, 1)
                act.wait_ge(y_weighted, g + 1)
                act.wait_ge(slots_hi_ready, taken)
                act.wait_ge(slots_lo_ready, taken)
                copy(pair_hi[1][:, :], merged_flat[:, 0:D]).then_inc(y_hi_ready, 1)

            def step(i, g, y=None, last_turn=False):
                more = (EXPERT_UNITS, g)
                if y is not None and i == 1:
                    weigh_y(y, EXPERT_UNITS * g + moe_unit(1, 0), g + 1)
                ahead(moe_unit(i, 0), more)
                ahead(moe_unit(i, 1), more)
                act.wait_ge(h_turned, TURNS_BEFORE + SLABS * g + i)
                copy(act_hi[:, :], bank[2][:, 0:256]).then_inc(act_hi_ready, 1)
                if i == 7 and not last_turn:
                    gathered_hi(g + 1, g - 1)
                if i == 10 and not last_turn:
                    take_slots(g + 1, EXPERT_UNITS * g + (moe_unit(10, 1) + 1))
                if i < 10 or not last_turn:
                    ahead(moe_unit(i, 2), more)
                silu(i, g)

            act.wait_ge(route_ready, 1)
            n_pass = act.value_load(n_pass_i[0:1, 0:1], min_val=1, max_val=2)
            with act.Fori(0, n_pass) as r:
                g0 = EXPERTS * r
                split_hi(act, UNITS1, (EXPERT_UNITS, g0))
                split_hi(act, UNITS1 + 1, (EXPERT_UNITS, g0))
                gathered_hi(g0)
                take_slots(g0, EXPERT_UNITS * g0 + UNITS1)
                ahead(UNITS1, (EXPERT_UNITS, g0))
                ahead(UNITS1 + 1, (EXPERT_UNITS, g0))
                silu(0, g0)
                for i in range(1, 6):
                    step(i, g0)
                with act.Fori(0, EXPERTS - 1) as e:
                    g = EXPERTS * r + e
                    for i in range(6, SLABS + 1):
                        step(i, g)
                    for i in range(1, 6):
                        step(i, g + 1, y=g)
                g7 = EXPERTS * r + (EXPERTS - 1)
                for i in range(6, SLABS):
                    step(i, g7, last_turn=True)
                act.wait_ge(h_turned, TURNS_BEFORE + SLABS * g7 + SLABS)
                copy(act_hi[:, :], bank[2][:, 0:256]).then_inc(act_hi_ready, 1)
                weigh_y(g7, EXPERT_UNITS * g7 + (moe_unit(SLABS, 0) + 1), g7 + 1)
                act.wait_ge(x_updated, X_BEFORE + 4 * g7 + 4)
            norm(4)
            for b in range(TB):
                act.wait_ge(out_scaled, b + 1)
                act.dma_start(out[:, b, :], xn[:, b, :]).then_inc(out_stored, 16)
            act.wait_ge(out_stored, 16 * TB)

        @block.vector
        def _(dve):
            steps = [0]

            def link(ins):
                steps[0] += 1
                ins.then_inc(dve_step, 1)
                dve.wait_ge(dve_step, steps[0])

            def tt(dst, a, b, op):
                return nc.vector.tensor_tensor(dst, a, b, op)

            def ts(dst, a, s1, s2=None, op0=ALU.mult, op1=None):
                if op1 is None:
                    return nc.vector.tensor_scalar(dst, a, s1, None, op0)
                return nc.vector.tensor_scalar(dst, a, s1, s2, op0, op1)

            def stt(dst, a, s, b, op0, op1):
                return nc.vector.scalar_tensor_tensor(out=dst, in0=a, scalar=s, in1=b, op0=op0, op1=op1)

            def low(dst, src, hi):
                return tt(dst, src, hi.bitcast(F32), ALU.subtract)

            def ahead(s, more=0):
                split_lo(dve, s + 2, more)

            def norm(i):
                dve.wait_ge(squares_ready, i + 1)
                ts(stat[:, 2:4], stat[:, 0:2], 1.0 / D, EPS, ALU.mult, ALU.add).then_inc(variance_ready, 1)
                dve.wait_ge(variance_ready, i + 1)
                dve.wait_ge(root_ready, i + 1)
                link(nc.vector.reciprocal(stat[:, 6:8], stat[:, 4:6]))
                link(tt(stat[:, 8:10], stat[:, 6:8], stat[:, 6:8], ALU.mult))
                link(tt(stat[:, 10:12], stat[:, 8:10], stat[:, 2:4], ALU.mult))
                link(ts(stat[:, 10:12], stat[:, 10:12], -0.5, 1.5, ALU.mult, ALU.add))
                tt(stat[:, 12:14], stat[:, 10:12], stat[:, 6:8], ALU.mult).then_inc(rstd_ready, 1)
                dve.wait_ge(rstd_ready, i + 1)
                if i < 4:
                    ts(xn[:, 1, :], xs[:, 1, :], stat[:, 13:14]).then_inc(xn1_ready, 1)

            def turned_lo(i, gain):
                for k in range(DC):
                    dve.wait_ge(h_hi_ready, DC * i + k + 1)
                    stt(h_lo[:, k, :], bank[k][:, 0:T],
                        vec[:, gain + k:gain + k + 1], h_hi[:, k, :].bitcast(F32),
                        ALU.mult, ALU.subtract).then_inc(h_lo_ready, 1)

            def update_x(used):
                dve.wait_ge(unit_used, used)
                for q in range(4):
                    part = xs[:, q // 2, (q % 2) * 512:(q % 2) * 512 + 512]
                    tt(part, part, bank[4 + q][:, :], ALU.add).then_inc(x_updated, 1)

            def mixer(layer):
                u0 = mixer_base(layer)

                def unit_done(u):
                    dve.wait_ge(unit_used, u0 + u + 1)

                def scores(b):
                    keys = P * (b + 1)
                    per = 512 // keys
                    dve.wait_ge(scores_done, TB * layer + b + 1)
                    m = mask[:, 256 - keys:256].unsqueeze(1).to_broadcast([P, per, keys])
                    for q in range(HEADS // per):
                        last = stt(probs[:, q * per:(q + 1) * per, 0:keys],
                                   bank[4 + q][:, :].rearrange("p (h k) -> p h k", h=per), HD ** -0.5, m,
                                   ALU.mult, ALU.add)
                    link(last)
                    link(nc.vector.tensor_reduce(stat[:, 16:24], probs[:, :, 0:keys], AX.X, ALU.max))
                    sink = vec[:, V_SINK + HEADS * layer:V_SINK + HEADS * layer + HEADS]
                    link(tt(stat[:, 16:24], stat[:, 16:24], sink, ALU.max))
                    ts(stat[:, 24:32], stat[:, 16:24], -1.0)
                    tt(stat[:, 40:48], sink, stat[:, 16:24], ALU.subtract).then_inc(neg_max_ready, 1)

                def normalise(b):
                    keys = P * (b + 1)
                    dve.wait_ge(exps_ready, TB * layer + b + 1)
                    link(tt(stat[:, 56:64], stat[:, 32:40], stat[:, 48:56], ALU.add))
                    link(nc.vector.reciprocal(stat[:, 64:72], stat[:, 56:64]))
                    r = stat[:, 64:72].unsqueeze(2).to_broadcast([P, HEADS, keys])
                    tt(probs[:, :, 0:keys], probs[:, :, 0:keys], r, ALU.mult).then_inc(probs_ready, 1)

                def attention_lo(b):
                    dve.wait_ge(att_hi_ready, TB * layer + b + 1)

                    def block_of(a):
                        return a.rearrange("p (j t) -> p j t", j=4)[:, :, b * P:(b + 1) * P]

                    low(block_of(pair_lo[0][:, :]), bank[4][:, :].rearrange("p (j t) -> p j t", j=4),
                        block_of(pair_hi[0][:, :])).then_inc(att_lo_ready, 1)

                def branch_lo(turn, src):
                    dve.wait_ge(branch_hi_ready, 3 * layer + turn)
                    low(pair_lo[turn % 2][:, :], src, pair_hi[turn % 2][:, :]).then_inc(branch_lo_ready, 1)

                def conv():
                    z = t1.rearrange("p (c t) -> p c t", c=CT)
                    y = t2.rearrange("p (c t) -> p c t", c=CT)
                    for back in range(3):
                        for c in range(CT):
                            tap = V_CONV + 12 * layer + (2 - back) * CT + c
                            w = vec[:, tap:tap + 1]
                            if back == 0:
                                last = ts(y[:, c, :], z[:, c, :], w)
                            else:
                                last = stt(y[:, c, back:T], z[:, c, 0:T - back], w, y[:, c, back:T],
                                           ALU.mult, ALU.add)
                        link(last)

                def pool():
                    p = t1.rearrange("p (g t) -> p g t", g=CT)
                    dve.wait_ge(act_evac, ACT_EVACS * layer + 8)
                    src = p
                    for g in range(CT):
                        w = 1 << g
                        dst = pool_b if g % 2 else pool_a
                        nc.vector.tensor_copy(dst[:, g:CT, 0:w], src[:, g:CT, 0:w])
                        link(tt(dst[:, g:CT, w:T], src[:, g:CT, w:T], src[:, g:CT, 0:T - w], ALU.add))
                        src = dst
                    for g in range(CT):
                        acc = pool_b if g % 2 else pool_a
                        fix = vec[:, V_FIX + 16 * g:V_FIX + 16 * g + 16]
                        last = tt(acc[:, g, 0:16], acc[:, g, 0:16], fix, ALU.mult)
                    link(last)
                    for g in range(CT):
                        acc = pool_b if g % 2 else pool_a
                        last = stt(p[:, g, :], acc[:, g, :], 1.0 / (2 << g), p[:, g, :], ALU.mult, ALU.subtract)
                    last.then_inc(pooled_ready, 1)

                norm(2 * layer)
                turned_lo(2 * layer, V_MIX_G + DC * layer)
                for u in range(5):
                    ahead(u0 + u)
                scores(0)
                ahead(u0 + 5)
                unit_done(5)
                dve.wait_ge(act_evac, ACT_EVACS * layer + 5)
                tt(t1[:, 0:512], t1[:, 0:512], bank[2][:, :], ALU.mult).then_inc(dve_evac, 1)
                normalise(0)
                ahead(u0 + 6)
                unit_done(6)
                tt(t1[:, 512:1024], t1[:, 512:1024], bank[0][:, :], ALU.mult).then_inc(dve_evac, 1)
                dve.wait_ge(dve_evac, DVE_EVACS * layer + 2)
                conv()
                ahead(u0 + 7)
                unit_done(7)
                tt(t1[:, 0:512], t2[:, 0:512], bank[1][:, :], ALU.mult).then_inc(dve_evac, 1)
                attention_lo(0)
                ahead(u0 + 8)
                unit_done(8)
                tt(t1[:, 512:1024], t2[:, 512:1024], bank[2][:, :], ALU.mult).then_inc(dve_evac, 1)
                dve.wait_ge(dve_evac, DVE_EVACS * layer + 4)
                scores(1)
                ahead(u0 + 9)
                normalise(1)
                ahead(u0 + 10)
                branch_lo(1, t1)
                ahead(u0 + 11)
                dve.wait_ge(branch_lo_ready, 3 * layer + 1)
                dve.wait_ge(mixed_done, layer + 1)
                for g in range(4):
                    b7 = bank[7 if g < 2 else 3][:, (g % 2) * T:(g % 2) * T + T].rearrange("p (b t) -> p b t", b=TB)
                    last = tt(t1[:, g * T:(g + 1) * T].rearrange("p (b t) -> p b t", b=TB), b7,
                              sgu_bias[:, g, :].unsqueeze(1).to_broadcast([P, TB, P]), ALU.add)
                last.then_inc(mixed_ready, 1)
                dve.wait_ge(mixed_ready, layer + 1)
                unit_done(11)
                tt(t3[:, 0:512], t1[:, 0:512], bank[2][:, :], ALU.mult).then_inc(dve_evac, 1)
                ahead(u0 + 12)
                unit_done(12)
                tt(t3[:, 512:1024], t1[:, 512:1024], bank[0][:, :], ALU.mult).then_inc(dve_evac, 1)
                ahead(u0 + 13)
                ahead(u0 + 14)
                for turn in range(BRANCHES):
                    for half in range(2):
                        u = PROJ_UNITS + 6 * turn + 3 * half
                        ahead(u0 + u)
                        if turn == 0 and half == 0:
                            attention_lo(1)
                        ahead(u0 + u + 1)
                        if turn == 0 and half == 0:
                            pool()
                        if turn == 1 and half == 0:
                            dve.wait_ge(pool_done, layer + 1)
                            for g in range(CT):
                                col = V_POOL + CT * layer + g
                                last = ts(t2[:, g * T:(g + 1) * T], bank[6 + g // 2][:, (g % 2) * T:(g % 2) * T + T],
                                          vec[:, col:col + 1])
                            last.then_inc(pool_scaled, 1)
                        if turn == BRANCHES - 1 and half == 1:
                            dve.wait_ge(merged_hi_ready, 2 * layer + 1)
                            low(h_lo_flat[:, 0:1024], merged_flat[:, 0:1024],
                                h_hi_flat[:, 0:1024]).then_inc(merged_lo_ready, 1)
                        ahead(u0 + u + 2)
                        if half == 0 and turn in (1, 2):
                            branch_lo(turn + 1, t3 if turn == 1 else t2)
                        unit_done(u + 2)
                        for q in range(2):
                            n = 4 * turn + 2 * half + q
                            dve.wait_ge(act_evac, ACT_EVACS * layer + 9 + n)
                            dst = merged_flat[:, (2 * half + q) * 512:(2 * half + q) * 512 + 512]
                            if turn == 0:
                                tt(dst, bank[4 + q][:, :], gate_buf[:, q, :], ALU.mult).then_inc(gate_used, 1)
                            else:
                                link(tt(gate_buf[:, q, :], bank[4 + q][:, :], gate_buf[:, q, :], ALU.mult))
                                dve.wait_ge(gate_used, 16 * layer + 4 * (turn - 1) + 2 * half + q + 1)
                                tt(dst, dst, gate_buf[:, q, :], ALU.add).then_inc(gate_used, 1)
                dve.wait_ge(merged_hi_ready, 2 * layer + 2)
                low(h_lo_flat[:, 1024:2048], merged_flat[:, 1024:2048],
                    h_hi_flat[:, 1024:2048]).then_inc(merged_lo_ready, 1)
                for u in range(MIX_UNITS - OUT_UNITS, MIX_UNITS):
                    if u0 + u + 2 < UNITS1:
                        ahead(u0 + u)
                update_x(u0 + MIX_UNITS)

            def dense():
                base = MIX_UNITS
                norm(1)
                turned_lo(1, V_FFN_G)

                def product(parity, n, used):
                    dve.wait_ge(silu_ready, n)
                    dve.wait_ge(unit_used, used)
                    tt(gate_buf[:, parity, :], gate_buf[:, parity, :], bank[2 + parity][:, :],
                       ALU.mult).then_inc(act_ready, 1)

                def split_product(parity, n):
                    dve.wait_ge(act_hi_ready, n)
                    low(pair_lo[parity][:, 0:512], gate_buf[:, parity, :],
                        pair_hi[parity][:, 0:512]).then_inc(act_lo_ready, 1)

                ahead(base)
                ahead(base + 1)
                product(0, 1, base + 2)
                with dve.Fori(0, (SLABS - 1) // 2) as it:
                    for j in range(2):
                        i = 1 + j
                        s = base + 2 + 3 * j
                        more = (6, it)
                        ahead(s, more)
                        split_product(j, 2 * it + i)
                        ahead(s + 1, more)
                        ahead(s + 2, more)
                        product(i % 2, 2 * it + (i + 1), 6 * it + (s + 2))
                split_product(0, SLABS)
                ahead(base + DENSE_UNITS - 1)
                update_x(base + DENSE_UNITS)

            dve.wait_ge(vec_loaded, 16)
            nc.vector.tensor_copy(ident_r[:, :], ident).then_inc(ident_ready, 1)
            split_lo(dve, 0)
            split_lo(dve, 1)
            mixer(0)
            dense()
            mixer(1)

            norm(3)
            dve.wait_ge(gain_loaded, 16)
            for b in range(TB):
                dve.wait_ge(xn0_ready if b == 0 else xn1_ready, 4)
                tt(xn[:, b, :], xn[:, b, :], gain_row, ALU.mult).then_inc(moe_h_ready, 1)
            for b in range(TB):
                dve.wait_ge(moe_h_hi_ready, b + 1)
                low(h_lo_flat[:, b * D:(b + 1) * D], xn[:, b, :],
                    h_hi_flat[:, b * D:(b + 1) * D]).then_inc(moe_h_lo_ready, 1)
            for half in range(2):
                dst = gate_flat if half == 0 else gain_row
                for q in range(2):
                    dve.wait_ge(r_turned, 2 * half + q + 1)
                    nc.vector.tensor_copy(dst[:, q * 512:(q + 1) * 512], bank[2 * half + q][:, :]).then_inc(r_copied, 1)
            dve.wait_ge(tables_loaded, 16)
            dve.wait_ge(logits_done, 2)

            def r(a, n=16):
                return route[:, a:a + n]

            def by_expert(a):
                return a.rearrange("p (b e) -> p b e", b=TB)

            def spread(a):
                return route[:, a:a + TB].unsqueeze(2).to_broadcast([P, TB, EXPERTS])

            rank = rank8.unsqueeze(1).to_broadcast([P, TB, EXPERTS])
            for b in range(TB):
                last = tt(r(EXPERTS * b, EXPERTS), bank[4 + b][:, 0:EXPERTS], vec[:, V_RB:V_RB + EXPERTS], ALU.add)
            link(last)

            def choose(values, top, chosen):
                link(nc.vector.tensor_reduce(r(top, TB), by_expert(r(values)), AX.X, ALU.max))
                link(tt(by_expert(r(16)), by_expert(r(values)), spread(top), ALU.is_equal))
                link(tt(by_expert(r(16)), by_expert(r(16)), rank, ALU.mult))
                link(nc.vector.tensor_reduce(r(82, TB), by_expert(r(16)), AX.X, ALU.max))
                link(tt(by_expert(r(chosen)), by_expert(r(16)), spread(82), ALU.is_equal))

            choose(0, 80, 32)
            link(ts(r(64), r(32), -1.0, 1.0, ALU.mult, ALU.add))
            link(tt(r(64), r(64), r(0), ALU.mult))
            link(stt(r(64), r(32), -3e38, r(64), ALU.mult, ALU.add))
            choose(64, 84, 48)
            link(tt(r(112), r(32), r(48), ALU.add))
            tt(r(86, TB), r(84, TB), r(80, TB), ALU.subtract).then_inc(gap_ready, 1)
            dve.wait_ge(gap_ready, 1)
            dve.wait_ge(exp_gap_ready, 1)
            link(ts(r(90, TB), r(88, TB), 1.0, None, ALU.add))
            link(nc.vector.reciprocal(r(92, TB), r(90, TB)))
            link(tt(r(94, TB), r(88, TB), r(92, TB), ALU.mult))
            link(tt(by_expert(r(96)), by_expert(r(32)), spread(92), ALU.mult))
            link(tt(by_expert(r(16)), by_expert(r(48)), spread(94), ALU.mult))
            link(tt(r(96), r(96), r(16), ALU.add))
            for half in range(2):
                last = nc.vector.tensor_copy(combine_r[:, :, 8 * half:8 * half + 8, 0], by_expert(r(96)))
            link(last)
            for half in range(2):
                last = tt(combine_r[:, :, 8 * half:8 * half + 8, 1], by_expert(r(96)),
                          combine_r[:, :, 0:8, 0].bitcast(F32), ALU.subtract)
            link(last)
            dve.wait_ge(places_done, 1)
            places = r(128, 32).rearrange("p (b g) -> p b g", b=TB)
            link(stt(places[:, :, 0:8], by_expert(bank[6][:, 0:16]), 1.0, by_expert(r(112)), ALU.add, ALU.mult))
            link(ts(places[:, :, 0:8], places[:, :, 0:8], 1.0, None, ALU.subtract))
            link(ts(places[:, :, 8:16], places[:, :, 0:8], float(P), None, ALU.subtract))
            link(nc.vector.tensor_reduce(r(200, 1), bank[6][:, 16:24], AX.X, ALU.max))
            link(ts(r(201, 1), r(200, 1), P + 0.5, 1.0, ALU.is_ge, ALU.add))
            nc.vector.tensor_copy(n_pass_i[:, :], r(201, 1)).then_inc(route_ready, 1)
            dve.wait_ge(route_ready, 1)

            def choose_slots(g, first=False):
                if not first:
                    dve.wait_ge(onehot_turned, g)
                    dve.wait_ge(gathered, g)
                for b in range(TB):
                    place = route[:, bass.ds(g + (128 + 16 * b), 1)]
                    last = nc.vector.tensor_scalar(onehot[:, b, :], iota, place, None, ALU.is_equal)
                last.then_inc(onehot_ready, 1)

            def gathered_lo(g):
                dve.wait_ge(next_hi_ready, g + 1)
                for q in range(2):
                    last = low(pair_lo[1][:, q * 512:(q + 1) * 512], bank[5 + q][:, :],
                               pair_hi[1][:, q * 512:(q + 1) * 512])
                last.then_inc(next_lo_ready, 1)

            def take_slots(g, used):
                dve.wait_ge(unit_used, used)
                dve.wait_ge(next_lo_ready, g + 1)
                nc.vector.tensor_copy(pair_lo[0][:, :], pair_lo[1][:, :].bitcast(F32)).then_inc(slots_lo_ready, 1)

            def split_y(g):
                dve.wait_ge(y_hi_ready, g + 1)
                low(pair_lo[1][:, :], merged_flat[:, 0:D], pair_hi[1][:, :]).then_inc(y_lo_ready, 1)

            def turned_onehot(g):
                dve.wait_ge(onehot_turned, g + 1)
                nc.vector.tensor_copy(onehot_t[:, :], bank[7][:, 0:T]).then_inc(onehot_t_ready, 1)
                nc.vector.tensor_reduce(stat[:, 60:61], bank[7][:, T:T + 2], AX.X, ALU.add).then_inc(share_ready, 1)

            def add_scattered(g, q):
                dve.wait_ge(scattered, 4 * g + q + 1)
                dve.wait_ge(x_updated, X_BEFORE + 4 * g)
                part = xs[:, q // 2, (q % 2) * 512:(q % 2) * 512 + 512]
                tt(part, part, bank[7][:, :], ALU.add).then_inc(x_updated, 1)

            def product(i, g):
                dve.wait_ge(silu_ready, SLABS * (g + 1) + i + 1)
                tt(gate_flat[:, 0:256], gate_flat[:, 0:256], slab_bank(i)[:, 256:512],
                   ALU.mult).then_inc(act_ready, 1)

            def slab_lo(i, g):
                dve.wait_ge(act_hi_ready, SLABS * (g + 1) + i + 1)
                low(act_lo[:, :], bank[2][:, 0:256], act_hi[:, :]).then_inc(act_lo_ready, 1)

            def step(i, g, y=None, last_turn=False):
                more = (EXPERT_UNITS, g)
                ahead(moe_unit(i, 0), more)
                if i == 8 and not last_turn:
                    gathered_lo(g + 1)
                ahead(moe_unit(i, 1), more)
                slab_lo(i - 1, g)
                if i == 10 and not last_turn:
                    take_slots(g + 1, EXPERT_UNITS * g + (moe_unit(10, 1) + 1))
                if i < 10 or not last_turn:
                    ahead(moe_unit(i, 2), more)
                product(i, g)
                if y is not None:
                    if i == 1:
                        split_y(y)
                    else:
                        add_scattered(y, i - 2)
                if i == 6:
                    turned_onehot(g)
                    if not last_turn:
                        choose_slots(g + 1)

            n_pass = dve.value_load(n_pass_i[0:1, 0:1], min_val=1, max_val=2)
            with dve.Fori(0, n_pass) as rr:
                g0 = EXPERTS * rr
                choose_slots(g0, first=True)
                split_lo(dve, UNITS1, (EXPERT_UNITS, g0))
                split_lo(dve, UNITS1 + 1, (EXPERT_UNITS, g0))
                gathered_lo(g0)
                take_slots(g0, EXPERT_UNITS * g0 + UNITS1)
                ahead(UNITS1, (EXPERT_UNITS, g0))
                ahead(UNITS1 + 1, (EXPERT_UNITS, g0))
                product(0, g0)
                for i in range(1, 6):
                    step(i, g0)
                with dve.Fori(0, EXPERTS - 1) as e:
                    g = EXPERTS * rr + e
                    for i in range(6, SLABS + 1):
                        step(i, g)
                    for i in range(1, 6):
                        step(i, g + 1, y=g)
                g7 = EXPERTS * rr + (EXPERTS - 1)
                for i in range(6, SLABS):
                    step(i, g7, last_turn=True)
                slab_lo(SLABS - 1, g7)
                split_y(g7)
                for q in range(4):
                    add_scattered(g7, q)
                dve.wait_ge(x_updated, X_BEFORE + 4 * g7 + 4)
            norm(4)
            dve.wait_ge(final_gain_loaded, 16)
            for b in range(TB):
                stt(xn[:, b, :], xs[:, b, :], stat[:, 12 + b:13 + b], gain_row, ALU.mult,
                    ALU.mult).then_inc(out_scaled, 1)

        @block.tensor
        def _(pe):
            def mm(dst, lhs_t, rhs, start, stop):
                return nc.tensor.matmul(dst, lhs_t, rhs, start=start, stop=stop)

            def mm3(dst, a, b, start, stop):
                mm(dst, a[0], b[0], start, False)
                mm(dst, a[0], b[1], False, False)
                return mm(dst, a[1], b[0], False, stop)

            def weights(s, more, cols):
                return w_hi[:, s % SPLIT_SLOTS, cols], w_lo[:, s % SPLIT_SLOTS, cols]

            def await_split(s, more=0):
                pe.wait_ge(hi_ready, at(s + 1, more))
                pe.wait_ge(lo_ready, at(s + 1, more))

            def h_part(k, lo=0, n=T):
                return h_hi[:, k, lo:lo + n], h_lo[:, k, lo:lo + n]

            def pair_part(i, lo, n):
                return pair_hi[i][:, lo:lo + n], pair_lo[i][:, lo:lo + n]

            def turn_rows(i):
                pe.wait_ge(vec_loaded, 16)
                pe.wait_ge(xn0_ready, i + 1)
                pe.wait_ge(xn1_ready, i + 1)
                for k in range(DC):
                    for b in range(TB):
                        last = nc.tensor.transpose(bank[k][:, b * P:(b + 1) * P], xn[:, b, k * P:(k + 1) * P], ident)
                    last.then_inc(h_turned, 1)

            def project(s, dst, tiles=2, norm_no=None, more=0):
                await_split(s, more)
                for t in range(tiles):
                    for k in range(DC):
                        if norm_no is not None and t == 0:
                            pe.wait_ge(h_lo_ready, DC * norm_no + k + 1)
                        last = mm3(dst[:, t * T:(t + 1) * T], weights(s, more, slice(k * T + t * P, k * T + (t + 1) * P)),
                                   h_part(k), k == 0, k == DC - 1)
                return last.then_inc(unit_used, 1)

            def mixer(layer):
                u0 = mixer_base(layer)

                def acts(n):
                    pe.wait_ge(act_evac, ACT_EVACS * layer + n)

                def dves(n):
                    pe.wait_ge(dve_evac, DVE_EVACS * layer + n)

                def scores(b):
                    keys = P * (b + 1)
                    per = 512 // keys
                    for h in range(HEADS):
                        half = slice(HD * (h // 4), HD * (h // 4) + HD)
                        last = mm(bank[4 + h // per][:, (h % per) * keys:(h % per + 1) * keys],
                                  q_t[half, h % 4, b * P:(b + 1) * P], k_t[half, 0:keys], True, True)
                    last.then_inc(scores_done, 1)

                def turn_probs(part):
                    pe.wait_ge(probs_ready, TB * layer + (2 if part else 1))
                    if 3 * layer + part:
                        pe.wait_ge(probs_t_ready, 3 * layer + part)
                    for n in range(8):
                        h, kb = (n, 0) if part == 0 else (4 * (part - 1) + n // 2, n % 2)
                        last = nc.tensor.transpose(bank[5 + n // 4][:, (n % 4) * P:(n % 4 + 1) * P],
                                                   probs[:, h, kb * P:(kb + 1) * P], ident)
                    last.then_inc(probs_turned, 1)

                def values(part):
                    pe.wait_ge(probs_t_ready, 3 * layer + part + 1)
                    blocks = 1 if part == 0 else 2
                    for h in range(HEADS) if part == 0 else range(4 * (part - 1), 4 * part):
                        half = slice(HD * (h // 4), HD * (h // 4) + HD)
                        for kb in range(blocks):
                            n = (h if part == 0 else (h % 4) * 2 + kb) * P
                            last = mm(bank[4][half, (h % 4) * P:(h % 4 + 1) * P], v_nat[:, kb, half],
                                      probs_t[:, n:n + P], kb == 0, kb == blocks - 1)
                    last.then_inc(att_half_done if part == 1 else att_done, 1)

                turn_rows(2 * layer)
                project(u0 + 0, bank[0][:, :], norm_no=2 * layer)
                project(u0 + 1, bank[1][:, :])
                project(u0 + 2, bank[2][:, :])
                acts(1)
                project(u0 + 3, bank[0][:, :])
                acts(3)
                for b in range(TB):
                    last = nc.tensor.transpose(bank[3][:, b * P:(b + 1) * P], v_t[:, b * P:(b + 1) * P], ident)
                last.then_inc(v_turned, 1)
                scores(0)
                project(u0 + 4, bank[1][:, :])
                project(u0 + 5, bank[2][:, :])
                acts(4)
                project(u0 + 6, bank[0][:, :])
                turn_probs(0)
                acts(5)
                project(u0 + 7, bank[1][:, :])
                pe.wait_ge(v_ready, layer + 1)
                values(0)
                dves(1)
                project(u0 + 8, bank[2][:, :])
                pe.wait_ge(att_lo_ready, TB * layer + 1)
                scores(1)
                for j in range(2):
                    await_split(u0 + 9 + j)
                    if j == 0:
                        dves(3)
                    for b in range(TB):
                        for kk in range(4):
                            k = 4 * j + kk
                            last = mm3(bank[b][:, :], h_part(k, b * P, P),
                                       weights(u0 + 9 + j, 0, slice(kk * 512, kk * 512 + 512)), k == 0, k == DC - 1)
                    last.then_inc(unit_used, 1)
                turn_probs(1)
                dves(4)
                project(u0 + 11, bank[2][:, :])
                values(1)
                acts(6)
                pe.wait_ge(sgu_masked, layer + 1)
                for g in range(4):
                    for b in range(TB):
                        last = mm(bank[7 if g < 2 else 3][:, (g % 2) * T + b * P:(g % 2) * T + (b + 1) * P],
                                  t3[:, b * 512 + g * P:b * 512 + (g + 1) * P], sgu_wt[:, g, :], True, True)
                last.then_inc(mixed_done, 1)
                project(u0 + 12, bank[0][:, :])
                turn_probs(2)
                project(u0 + 13, bank[1][:, :])
                dves(5)
                project(u0 + 14, bank[2][:, :])
                values(2)
                for turn in range(BRANCHES):
                    for half in range(2):
                        u = PROJ_UNITS + 6 * turn + 3 * half
                        for q in range(2):
                            if turn:
                                acts(9 + 4 * (turn - 1) + 2 * half + q)
                            elif half == 0:
                                dves(6) if q == 0 else acts(7)
                            else:
                                acts(8) if q == 0 else pe.wait_ge(mixed_ready, layer + 1)
                            project(u0 + u + q, bank[2 * half + q][:, :])
                        await_split(u0 + u + 2)
                        if turn == 0:
                            pe.wait_ge(att_lo_ready, TB * (layer + 1))
                        else:
                            pe.wait_ge(branch_lo_ready, 3 * layer + turn)
                        if turn or half:
                            pe.wait_ge(gate_used, 16 * layer + 4 * turn + 2 * half)
                        for t in range(4):
                            for c in range(CT):
                                last = mm3(bank[4 + t // 2][:, (t % 2) * T:(t % 2) * T + T],
                                           weights(u0 + u + 2, 0, slice(c * 512 + t * P, c * 512 + (t + 1) * P)),
                                           pair_part(turn % 2, c * T, T), c == 0, c == CT - 1)
                        last.then_inc(unit_used, 1)
                        if turn == 0 and half == 1:
                            pe.wait_ge(pooled_ready, layer + 1)
                            for g in range(CT):
                                last = mm(bank[6 + g // 2][:, (g % 2) * T:(g % 2) * T + T], pool_w[:, g, :],
                                          t1[:, g * T:(g + 1) * T], True, True)
                            last.then_inc(pool_done, 1)
                for j in range(OUT_UNITS):
                    s = u0 + MIX_UNITS - OUT_UNITS + j
                    await_split(s)
                    pe.wait_ge(merged_lo_ready, 2 * layer + 1 + j // 2)
                    if j == 0:
                        pe.wait_ge(gate_used, 16 * layer + 16)
                        pe.wait_ge(pool_scaled, layer + 1)
                    for kk in range(2):
                        k = 2 * j + kk
                        for b in range(TB):
                            for half in range(2):
                                cols = slice(kk * D + half * 512, kk * D + half * 512 + 512)
                                last = mm3(bank[4 + 2 * b + half][:, :], h_part(k, b * P, P),
                                           weights(s, 0, cols), k == 0, k == DC - 1)
                    last.then_inc(unit_used, 1)

            def dense():
                base = MIX_UNITS

                def down(s, parity, n, first=False, more=0, complete=False):
                    await_split(s, more)
                    pe.wait_ge(act_lo_ready, n)
                    for f in range(2):
                        for b in range(TB):
                            for half in range(2):
                                cols = slice(f * D + half * 512, f * D + half * 512 + 512)
                                last = mm3(bank[4 + 2 * b + half][:, :], pair_part(parity, f * T + b * P, P),
                                           weights(s, more, cols), first and f == 0, complete and f == 1)
                    last.then_inc(unit_used, 1)

                turn_rows(1)
                project(base, bank[0][:, :], norm_no=1)
                project(base + 1, bank[2][:, :])
                project(base + 2, bank[1][:, :])
                project(base + 3, bank[3][:, :])
                down(base + 4, 0, 1, True)
                pe.wait_ge(act_ready, 1)
                project(base + 5, bank[0][:, :])
                project(base + 6, bank[2][:, :])
                down(base + 7, 1, 2, False)
                with pe.Fori(1, (SLABS - 1) // 2) as it:
                    for j in range(2):
                        i = 1 + j
                        s = base + 2 + 3 * j
                        more = (6, it)
                        pe.wait_ge(act_ready, 2 * it + (i - 1))
                        project(s, bank[i % 2][:, :], more=more)
                        project(s + 1, bank[2 + i % 2][:, :], more=more)
                        down(s + 2, j, 2 * it + i, False, more)
                down(base + DENSE_UNITS - 1, 0, SLABS, False, complete=True)

            def router():
                pe.wait_ge(moe_h_ready, TB)
                for k in range(DC):
                    for b in range(TB):
                        last = nc.tensor.transpose(bank[k // 2][:, (k % 2) * T + b * P:(k % 2) * T + (b + 1) * P],
                                                   xn[:, b, k * P:(k + 1) * P], ident)
                    if k % 2:
                        last.then_inc(r_turned, 1)
                for half in range(2):
                    pe.wait_ge(r_copied, 2 * half + 2)
                    rows = gate_flat if half == 0 else gain_row
                    for kk in range(4):
                        k = 4 * half + kk
                        for b in range(TB):
                            last = mm(bank[4 + b][:, 0:EXPERTS], rows[:, kk * T + b * P:kk * T + (b + 1) * P],
                                      vec[:, V_RW + EXPERTS * k:V_RW + EXPERTS * (k + 1)], k == 0, k == DC - 1)
                    last.then_inc(logits_done, 1)
                pe.wait_ge(tables_loaded, 16)
                pe.wait_ge(gap_ready, 1)
                chosen = [route[:, 112 + EXPERTS * b:112 + EXPERTS * (b + 1)] for b in range(TB)]
                mm(bank[6][:, 0:8], earlier, chosen[0], True, True)
                mm(bank[6][:, 8:16], ones, chosen[0], True, False)
                mm(bank[6][:, 8:16], earlier, chosen[1], False, True)
                mm(bank[6][:, 16:24], ones, chosen[0], True, False)
                mm(bank[6][:, 16:24], ones, chosen[1], False, True).then_inc(places_done, 1)

            def gather(g, first=False):
                pe.wait_ge(onehot_ready, g + 1)
                if not first:
                    pe.wait_ge(next_lo_ready, g)
                pe.wait_ge(moe_h_lo_ready, TB)
                for k in range(DC):
                    dst = bank[5 + k // 4][:, (k % 4) * P:(k % 4 + 1) * P]
                    for b in range(TB):
                        rows = slice(b * D + k * P, b * D + (k + 1) * P)
                        mm(dst, h_hi_flat[:, rows], onehot[:, b, :], b == 0, False)
                        last = mm(dst, h_lo_flat[:, rows], onehot[:, b, :], False, b == TB - 1)
                last.then_inc(gathered, 1)

            def turn_onehot(g):
                pe.wait_ge(x_updated, X_BEFORE + 4 * g)
                pe.wait_ge(ident_ready, 1)
                for b in range(TB):
                    mm(bank[7][:, b * P:(b + 1) * P], onehot[:, b, :], ident_r[:, :], True, True)
                for b in range(TB):
                    share = combine_r[:, b, bass.ds(g, 1), :].rearrange("p g c -> p (g c)")
                    last = mm(bank[7][:, T:T + 2], onehot[:, b, :], share, b == 0, b == TB - 1)
                last.then_inc(onehot_turned, 1)

            def scatter(g, q):
                pe.wait_ge(y_lo_ready, g + 1)
                pe.wait_ge(onehot_t_ready, g + 1)
                pe.wait_ge(x_updated, X_BEFORE + 4 * g + q)
                tokens = onehot_t[:, (q // 2) * P:(q // 2 + 1) * P]
                cols = slice((q % 2) * 512, (q % 2) * 512 + 512)
                mm(bank[7][:, :], tokens, pair_hi[1][:, cols], True, False)
                mm(bank[7][:, :], tokens, pair_lo[1][:, cols], False, True).then_inc(scattered, 1)

            def gate_up(i, j, g):
                s = moe_unit(i, j)
                await_split(s, (EXPERT_UNITS, g))
                for kk in range(4):
                    k = 4 * j + kk
                    last = mm3(slab_bank(i)[:, :], pair_part(0, k * P, P),
                               weights(s, 0, slice(kk * 512, kk * 512 + 512)), k == 0, k == DC - 1)
                last.then_inc(unit_used, 1)

            def turn_slab(i, g):
                pe.wait_ge(act_ready, SLABS * (g + 1) + i + 1)
                pe.wait_ge(act_lo_ready, SLABS * (g + 1) + i)
                for f in range(2):
                    last = nc.tensor.transpose(bank[2][:, f * P:(f + 1) * P], gate_flat[:, f * P:(f + 1) * P], ident)
                last.then_inc(h_turned, 1)

            def down_slab(i, g, y=None, last_turn=False):
                s = moe_unit(i + 1, 0 if last_turn and i == SLABS - 1 else 2)
                await_split(s, (EXPERT_UNITS, g))
                pe.wait_ge(act_lo_ready, SLABS * (g + 1) + i + 1)
                if i == 0 and y is not None:
                    pe.wait_ge(y_weighted, y + 1)
                for f in range(2):
                    for half in range(2):
                        cols = slice(f * D + half * 512, f * D + half * 512 + 512)
                        last = mm3(bank[3 + half][:, :], (act_hi[:, f * P:(f + 1) * P], act_lo[:, f * P:(f + 1) * P]),
                                   weights(s, 0, cols), i == 0 and f == 0, i == SLABS - 1 and f == 1)
                last.then_inc(unit_used, 1)

            def step(i, g, y=None, last_turn=False):
                if i == SLABS:
                    pe.wait_ge(slots_hi_ready, g + 2)
                    pe.wait_ge(slots_lo_ready, g + 2)
                pe.wait_ge(act_ready, SLABS * (g + 1) + (i - 1))
                gate_up(i, 0, g)
                turn_slab(i - 1, g)
                gate_up(i, 1, g)
                if y is not None and i >= 2:
                    scatter(y, i - 2)
                if i == 6:
                    turn_onehot(g)
                if i == 7 and not last_turn:
                    gather(g + 1)
                down_slab(i - 1, g, y)

            mixer(0)
            dense()
            mixer(1)
            router()
            pe.wait_ge(route_ready, 1)
            n_pass = pe.value_load(n_pass_i[0:1, 0:1], min_val=1, max_val=2)
            with pe.Fori(0, n_pass) as r:
                g0 = EXPERTS * r
                gather(g0, first=True)
                pe.wait_ge(slots_hi_ready, g0 + 1)
                pe.wait_ge(slots_lo_ready, g0 + 1)
                gate_up(0, 0, g0)
                gate_up(0, 1, g0)
                for i in range(1, 6):
                    step(i, g0)
                with pe.Fori(0, EXPERTS - 1) as e:
                    g = EXPERTS * r + e
                    for i in range(6, SLABS + 1):
                        step(i, g)
                    for i in range(1, 6):
                        step(i, g + 1, y=g)
                g7 = EXPERTS * r + (EXPERTS - 1)
                for i in range(6, SLABS):
                    step(i, g7, last_turn=True)
                turn_slab(SLABS - 1, g7)
                down_slab(SLABS - 1, g7, last_turn=True)
                for q in range(4):
                    scatter(g7, q)
                pe.wait_ge(x_updated, X_BEFORE + 4 * g7 + 4)



def kernel(**inputs):
    import numpy as np
    import concourse.bacc as bacc
    from concourse.bass_utils import run_bass_kernel_spmd

    a = {k: np.asarray(v) for k, v in inputs.items()}

    def still(w):
        return w.reshape(DC, P, 256).transpose(1, 0, 2).reshape(1, P, UNIT)

    def moving(w, cols):
        n = UNIT // cols
        return w.reshape(-1, n, P, cols).transpose(0, 2, 1, 3).reshape(-1, P, UNIT)

    paired = np.concatenate([np.r_[HD * j:HD * j + HD, 256 + HD * j:256 + HD * j + HD] for j in range(4)])

    def mixer_units(layer):
        w = a["w_in"][layer]
        out = [still(w[:, paired[0:256]]), still(w[:, paired[256:512]]), still(w[:, 512:768])]

        def two(start):
            return [still(w[:, start:start + 256]), still(w[:, start + 256:start + 512])]

        cb, cc, cx, p, u, sv, gates = 768, 1280, 1792, 2304, 2816, 3328, 3840
        out += two(cc) + two(cx) + two(cb) + [moving(w[:, sv:sv + 512], 512)] + two(u) + two(p)
        for branch in BRANCH_ORDER:
            wb = a["w_branch"][layer, branch]
            if branch == 0:
                wb = wb[paired]
            for half in range(2):
                out += two(gates + branch * D + half * 512)
                out.append(moving(wb[:, half * 512:half * 512 + 512], 512))
        out.append(moving(a["w_out"][layer], D))
        return out

    def dense_units():
        gate, up, down = (a[f"dense_w_{n}"][0] for n in ("gate", "up", "down"))
        downs = moving(down, D)
        out = []
        for i in range(SLABS):
            out += [still(gate[:, 256 * i:256 * i + 256]), still(up[:, 256 * i:256 * i + 256])]
            if i:
                out.append(downs[i - 1:i])
        return out + [downs[SLABS - 1:]]

    def moe_units():
        gate, up, down = (a[f"moe_w_{n}"][0] for n in ("gate", "up", "down"))
        s = np.empty((MOE_UNITS, P, UNIT), gate.dtype)
        at_unit = 0
        late = None
        for e in range(EXPERTS):
            downs = moving(down[e], D)
            for i in range(SLABS):
                cols = slice(256 * i, 256 * i + 256)
                s[at_unit:at_unit + 2] = moving(np.concatenate([gate[e][:, cols], up[e][:, cols]], 1), 512)
                at_unit += 2
                if late is not None:
                    s[at_unit] = late
                    at_unit += 1
                late = downs[i]
        s[at_unit] = late
        return s

    def spread(v):
        return np.broadcast_to(v.reshape(1, -1), (P, v.size))

    def by_chunk(v):
        return v.reshape(-1, P).T

    t = np.arange(P)
    keys = np.arange(2 * P)
    rel = t[:, None] + P - keys[None, :]
    mask = np.where((rel >= 0) & (rel < P), 0.0, NEG).astype(np.float32)
    fix = np.stack([(2 << g) / np.minimum(np.arange(16) + 1, 2 << g) for g in range(CT)]).astype(np.float32)
    small = np.concatenate([
        by_chunk(a["ln_mix_g"]), by_chunk(a["ln_ffn_g"]), by_chunk(a["conv_w"]), by_chunk(a["pool_scale"]),
        spread(a["attn_sinks"]), spread(a["router_b"][0]),
        a["router_w"][0].reshape(DC, P, EXPERTS).transpose(1, 0, 2).reshape(P, DC * EXPERTS),
        spread(fix), mask, np.eye(P, dtype=np.float32)], 1)
    tables = np.concatenate([
        spread(np.arange(P, dtype=np.float32)), np.triu(np.ones((P, P), np.float32), 1),
        np.ones((P, P), np.float32), spread(8 - np.arange(8, dtype=np.float32)), np.zeros((P, 120), np.float32)], 1)
    layer_weights = np.stack([np.concatenate([
        a["sgu_w"][n].transpose(2, 0, 1).reshape(P, 512), a["pool_w"][n].transpose(1, 0, 2).reshape(P, 512),
        spread(a["sgu_b"][n])], 1) for n in range(LAYERS)])
    gains = np.stack([spread(a["ln_ffn_g"][1]), spread(a["ln_final_g"])])
    arrays = {
        "x": a["x"].reshape(TB, P, D).transpose(1, 0, 2),
        "small": small,
        "tables": tables,
        "layer_weights": layer_weights,
        "gains": gains,
        "stream1": np.concatenate(mixer_units(0) + dense_units() + mixer_units(1)),
        "stream2": moe_units(),
    }
    arrays = {k: np.ascontiguousarray(v) for k, v in arrays.items()}
    nc = bacc.Bacc("TRN2", target_bir_lowering=False, num_devices=1)
    args = [nc.dram_tensor(n, v.shape, F32, kind="ExternalInput").ap() for n, v in arrays.items()]
    out = nc.dram_tensor("out", (T, D), F32, kind="ExternalOutput").ap()
    trunk(nc, *args, out.rearrange("(b p) d -> p b d", p=P))
    r = run_bass_kernel_spmd(nc, [arrays], core_ids=[0])
    return r.results[0]["out"].reshape(1, T, D)
```

```python
from contextlib import ExitStack

import concourse.bass as bass
from concourse import mybir

P = 128
D = 1024
T = 256
TB = T // P
DC = D // P
LAYERS = 2
HEADS = 8
HD = 64
BRANCHES = 4
CT = 4
FFN = 2816
EXPERTS = 8
EPS = 1e-6
NEG = -1e30

UNIT = 2048
HALF = UNIT // 2
HI_UNITS = 6
HI_HALVES = 11
AHEAD = 2
RAW1 = 6
RAW2 = 11
PROJ_UNITS = 15
GATE_UNITS = 3 * 2 * BRANCHES
OUT_UNITS = 4
MIX_UNITS = PROJ_UNITS + GATE_UNITS + OUT_UNITS
SLABS = FFN // 256
DENSE_UNITS = 3 * SLABS
UNITS1 = 2 * MIX_UNITS + DENSE_UNITS
MOE_UNITS = DENSE_UNITS * EXPERTS
EXPERT_UNITS = DENSE_UNITS

F32 = mybir.dt.float32
F32R = mybir.dt.float32r
I32 = mybir.dt.int32
ALU = mybir.AluOpType
ACT = mybir.ActivationFunctionType
AX = mybir.AxisListType

V_MIX_G, V_FFN_G = 0, 16
V_CONV, V_POOL, V_SINK = 32, 56, 64
V_RB = 80
V_RW = 88
V_FIX = V_RW + DC * EXPERTS
V_MASK = V_FIX + 16 * CT
V_IDENT = V_MASK + 256
V_COLS = V_IDENT + 128

ACT_EVACS = 24
DVE_EVACS = 6
X_BEFORE = 4 * (LAYERS + 1)
TURNS_BEFORE = DC * (LAYERS + 2)
BRANCH_ORDER = [0, 1, 3, 2]


def mixer_base(layer):
    return layer * (MIX_UNITS + DENSE_UNITS)


def at(n, more):
    return n + more[0] * more[1] if more else n


def loads(more, ring):
    return more[0] // ring * 16 * more[1] if more else 0


def trunk(nc, x, small, tables, layer_weights, gains, stream1, stream2, out):
    ctx = ExitStack()
    with ctx:
        def sb(name, shape, dt=F32):
            return ctx.enter_context(nc.sbuf_tensor(name, shape, dt))

        def next_place():
            return -(-nc.sbuf_base // 32) * 32

        def over(name, shape, dt, place):
            return nc.alloc_sbuf_tensor_at(name, shape, dt, offset=place)

        def sem(name):
            return ctx.enter_context(nc.semaphore(name))

        raw_at = next_place()
        raw = sb("raw", [P, RAW2, UNIT])
        w_lo = [over(f"w_lo{i}", [P, UNIT], F32R, raw_at + 4 * UNIT * i) for i in range(RAW2)]
        w_hi = sb("w_hi", [P, HI_UNITS * UNIT], F32R)
        xs = sb("xs", [P, TB, D])
        h_hi = sb("h_hi", [P, DC, T], F32R)
        h_lo = sb("h_lo", [P, DC, T], F32R)
        merged = sb("merged", [P, DC, T])
        gate_buf = sb("gate_buf", [P, 2, 512])
        pair_at = next_place()
        pair_hi = [sb(f"pair{i}_hi", [P, CT * T], F32R) for i in range(2)]
        pair_lo = [sb(f"pair{i}_lo", [P, CT * T], F32R) for i in range(2)]
        act_hi = sb("act_hi", [P, 2 * P], F32R)
        act_lo = sb("act_lo", [P, 2 * P], F32R)
        onehot = sb("onehot", [P, TB, P], F32R)
        onehot_t = sb("onehot_t", [P, TB * P], F32R)
        ident_r = sb("ident_r", [P, P], F32R)
        weights_small = sb("weights_small", [P, 1536])
        vec = sb("vec", [P, V_COLS])
        stat = sb("stat", [P, 128])
        route = sb("route", [P, 320])
        combine_r = sb("combine_r", [P, TB, 16, 2], F32R)
        n_pass_i = sb("n_pass_i", [P, 1], I32)

        bank = [ctx.enter_context(nc.psum_tensor(f"bank{i}", [P, 512], F32)) for i in range(8)]

        scratch = raw[:, RAW1:RAW2, :].rearrange("p s u -> p (s u)")
        t1, t2, t3 = (scratch[:, i * 1024:(i + 1) * 1024] for i in range(3))
        probs = scratch[:, 3072:5120].rearrange("p (h k) -> p h k", h=HEADS)
        probs_t = scratch[:, 5120:6144]
        pool_a = scratch[:, 6144:7168].rearrange("p (g t) -> p g t", g=CT)
        pool_b = scratch[:, 7168:8192].rearrange("p (g t) -> p g t", g=CT)
        qkv_s = scratch[:, 8192:9984]
        q_t = qkv_s[:, 0:1024].rearrange("p (j t) -> p j t", j=4)
        k_t = qkv_s[:, 1024:1280]
        v_t = qkv_s[:, 1280:1536]
        v_nat = qkv_s[:, 1536:1792].rearrange("p (b d) -> p b d", b=TB)
        merged_flat = merged[:, :, :].rearrange("p k t -> p (k t)")
        xn = merged_flat.rearrange("p (b d) -> p b d", b=TB)
        moe_rows_over = [over(f"moe_rows{b}", [P, D], F32, pair_at + 4 * D * b) for b in range(TB)]
        moe_rows = [rows[:, :] for rows in moe_rows_over]
        h_hi_flat = h_hi[:, :, :].rearrange("p k t -> p (k t)")
        h_lo_flat = h_lo[:, :, :].rearrange("p k t -> p (k t)")
        gate_flat = gate_buf[:, :, :].rearrange("p q c -> p (q c)")
        sgu_wt = weights_small[:, 0:512].rearrange("p (g t) -> p g t", g=4)
        pool_w = weights_small[:, 512:1024].rearrange("p (g t) -> p g t", g=4)
        sgu_bias = weights_small[:, 1024:1536].rearrange("p (g t) -> p g t", g=4)
        gain_row = weights_small[:, 0:1024]
        iota = weights_small[:, 1024:1152]
        earlier = weights_small[:, 1152:1280]
        ones = weights_small[:, 1280:1408]
        rank8 = weights_small[:, 1408:1416]
        ident = vec[:, V_IDENT:V_IDENT + P]
        mask = vec[:, V_MASK:V_MASK + 256]

        x_loaded = sem("x_loaded")
        vec_loaded = sem("vec_loaded")
        small_loaded = sem("small_loaded")
        tables_loaded = sem("tables_loaded")
        gain_loaded = sem("gain_loaded")
        final_gain_loaded = sem("final_gain_loaded")
        sgu_masked = sem("sgu_masked")
        landed1 = [sem(f"landed1_{i}") for i in range(RAW1)]
        landed2 = [sem(f"landed2_{i}") for i in range(RAW2)]
        hi_ready = sem("hi_ready")
        lo_ready = sem("lo_ready")
        unit_used = sem("unit_used")
        squares_ready = sem("squares_ready")
        variance_ready = sem("variance_ready")
        root_ready = sem("root_ready")
        rstd_ready = sem("rstd_ready")
        xn0_ready = sem("xn0_ready")
        xn1_ready = sem("xn1_ready")
        h_turned = sem("h_turned")
        h_hi_ready = sem("h_hi_ready")
        h_lo_ready = sem("h_lo_ready")
        act_evac = sem("act_evac")
        dve_evac = sem("dve_evac")
        v_turned = sem("v_turned")
        v_ready = sem("v_ready")
        scores_done = sem("scores_done")
        neg_max_ready = sem("neg_max_ready")
        exps_ready = sem("exps_ready")
        probs_ready = sem("probs_ready")
        probs_turned = sem("probs_turned")
        probs_t_ready = sem("probs_t_ready")
        att_done = sem("att_done")
        att_half_done = sem("att_half_done")
        att_hi_ready = sem("att_hi_ready")
        att_lo_ready = sem("att_lo_ready")
        pool_scaled = sem("pool_scaled")
        branch_hi_ready = sem("branch_hi_ready")
        branch_lo_ready = sem("branch_lo_ready")
        mixed_done = sem("mixed_done")
        mixed_ready = sem("mixed_ready")
        pooled_ready = sem("pooled_ready")
        pool_done = sem("pool_done")
        gate_used = sem("gate_used")
        merged_hi_ready = sem("merged_hi_ready")
        merged_lo_ready = sem("merged_lo_ready")
        sum0_done = sem("sum0_done")
        x_updated = sem("x_updated")
        silu_ready = sem("silu_ready")
        act_ready = sem("act_ready")
        act_hi_ready = sem("act_hi_ready")
        act_lo_ready = sem("act_lo_ready")
        r_copied = sem("r_copied")
        logits_done = sem("logits_done")
        gap_ready = sem("gap_ready")
        exp_gap_ready = sem("exp_gap_ready")
        ident_ready = sem("ident_ready")
        places_done = sem("places_done")
        route_ready = sem("route_ready")
        moe_h_ready = sem("moe_h_ready")
        moe_h_hi_ready = sem("moe_h_hi_ready")
        moe_h_lo_ready = sem("moe_h_lo_ready")
        onehot_ready = sem("onehot_ready")
        onehot_turned = sem("onehot_turned")
        onehot_t_ready = sem("onehot_t_ready")
        share_ready = sem("share_ready")
        gathered = sem("gathered")
        slots_hi_ready = sem("slots_hi_ready")
        slots_lo_ready = sem("slots_lo_ready")
        y_weighted = sem("y_weighted")
        y_hi_ready = sem("y_hi_ready")
        y_lo_ready = sem("y_lo_ready")
        scattered = sem("scattered")
        out_scaled = sem("out_scaled")
        out_stored = sem("out_stored")
        dve_step = sem("dve_step")


        def raw_slot(s):
            return s % RAW1 if s < UNITS1 else (s - UNITS1) % RAW2

        def raw_of(s):
            return raw[:, raw_slot(s), :]

        def lo_of(s):
            return w_lo[raw_slot(s)]

        def hi_half(s, half):
            n = 2 * s % (2 * HI_UNITS) if s < UNITS1 else 2 * (s - UNITS1) % HI_HALVES
            return (n + half) % (2 * HI_UNITS if s < UNITS1 else HI_HALVES) * HALF

        def pieces(s):
            if hi_half(s, 1) > hi_half(s, 0):
                return [(slice(0, UNIT), hi_half(s, 0))]
            return [(slice(0, HALF), hi_half(s, 0)), (slice(HALF, UNIT), hi_half(s, 1))]

        def split_hi(act, s, more=0):
            if s < UNITS1:
                act.wait_ge(landed1[s % RAW1], 16 * (s // RAW1 + 1) + loads(more, RAW1))
            else:
                act.wait_ge(landed2[(s - UNITS1) % RAW2], 16 * ((s - UNITS1) // RAW2 + 1) + loads(more, RAW2))
            if s >= HI_UNITS:
                act.wait_ge(unit_used, at(s - HI_UNITS + (1 if s < UNITS1 else 2), more))
            for cols, start in pieces(s):
                last = nc.scalar.activation(w_hi[:, start:start + cols.stop - cols.start], raw_of(s)[:, cols],
                                            ACT.Copy)
            last.then_inc(hi_ready, 1)

        def split_lo(dve, s, more=0):
            dve.wait_ge(hi_ready, at(s + 1, more))
            for cols, start in pieces(s):
                last = nc.vector.tensor_tensor(lo_of(s)[:, cols], raw_of(s)[:, cols],
                                               w_hi[:, start:start + cols.stop - cols.start].bitcast(F32),
                                               ALU.subtract)
            last.then_inc(lo_ready, 1)

        def moe_unit(i, k):
            return UNITS1 + 2 + 3 * (i - 1) + k if i else UNITS1 + k

        def slab_bank(i):
            return bank[7 if i % SLABS == 0 else i % 2]

        def scatter_bank(q, last_turn):
            return bank[(7, 0, 1, 5)[q] if last_turn else 7]

        block = ctx.enter_context(nc.Block())

        @block.sync
        def _(sp):
            sp.dma_start(vec[:, :], small).then_inc(vec_loaded, 16)
            sp.dma_start(xs[:, :, :], x).then_inc(x_loaded, 16)
            for s in range(RAW1):
                sp.dma_start(raw[:, s, :], stream1[s]).then_inc(landed1[s], 16)
            rounds = UNITS1 // RAW1
            with sp.Fori(1, rounds) as i:
                for s in range(RAW1):
                    sp.wait_ge(unit_used, (i - 1) * RAW1 + (s + 1))
                    sp.dma_start(raw[:, s, :], stream1[i * RAW1 + s]).then_inc(landed1[s], 16)
            for n in range(rounds * RAW1, UNITS1):
                sp.wait_ge(unit_used, n - RAW1 + 1)
                sp.dma_start(raw[:, n % RAW1, :], stream1[n]).then_inc(landed1[n % RAW1], 16)
            for m in range(RAW2):
                if m < RAW1:
                    sp.wait_ge(unit_used, max(n for n in range(UNITS1) if n % RAW1 == m) + 1)
                elif m == RAW1:
                    sp.wait_ge(branch_lo_ready, 3 * LAYERS)
                sp.dma_start(raw[:, m, :], stream2[m]).then_inc(landed2[m], 16)
            rounds = MOE_UNITS // RAW2
            with sp.Fori(1, rounds) as i:
                for s in range(RAW2):
                    sp.wait_ge(unit_used, (i - 1) * RAW2 + (UNITS1 + s + 1))
                    sp.dma_start(raw[:, s, :], stream2[i * RAW2 + s]).then_inc(landed2[s], 16)
            sp.wait_ge(route_ready, 1)
            n_pass = sp.value_load(n_pass_i[0:1, 0:1], min_val=1, max_val=2)
            with sp.If(n_pass > 1):
                with sp.Fori(rounds, 2 * rounds) as i:
                    for s in range(RAW2):
                        sp.wait_ge(unit_used, (i - 1) * RAW2 + (UNITS1 + s + 1))
                        sp.dma_start(raw[:, s, :], stream2[i * RAW2 + (s - MOE_UNITS)]).then_inc(landed2[s], 16)

        @block.gpsimd
        def _(pool):
            pool.dma_start(weights_small[:, :], layer_weights[0]).then_inc(small_loaded, 16)
            for layer in range(LAYERS):
                if layer:
                    pool.wait_ge(pool_done, layer)
                    pool.wait_ge(mixed_ready, layer)
                    pool.dma_start(weights_small[:, :], layer_weights[layer]).then_inc(small_loaded, 16)
                pool.wait_ge(small_loaded, 16 * (layer + 1))
                nc.gpsimd.affine_select(out=sgu_wt, in_=sgu_wt, compare_op=ALU.is_ge, fill=0.0, base=0,
                                        pattern=[[0, 4], [1, P]], channel_multiplier=-1).then_inc(sgu_masked, 1)
            pool.wait_ge(pool_done, LAYERS)
            pool.wait_ge(mixed_ready, LAYERS)
            pool.dma_start(weights_small[:, 1024:1536], tables).then_inc(tables_loaded, 16)
            pool.dma_start(gain_row, gains[0]).then_inc(gain_loaded, 16)
            pool.wait_ge(logits_done, 1)
            pool.dma_start(gain_row, gains[1]).then_inc(final_gain_loaded, 16)

        @block.scalar
        def _(act):
            def copy(dst, src, scale=1.0):
                return nc.scalar.activation(dst, src, ACT.Copy, scale=scale)

            def ahead(s, more=0, last_turn=False):
                if not (last_turn and s + AHEAD >= UNITS1 + EXPERT_UNITS):
                    split_hi(act, s + AHEAD, more)

            def norm(i, done=None):
                if i == 0:
                    act.wait_ge(vec_loaded, 16)
                nc.scalar.activation(stat[:, 72:73], ident[:, 0:1], ACT.Sqrt)
                if i == 0:
                    act.wait_ge(x_loaded, 16)
                for b in range(TB):
                    if 0 < i < 4:
                        act.wait_ge(x_updated, 4 * (i - 1) + 2 * b + 2)
                    elif i == 4:
                        act.wait_ge(x_updated, done + 2 * b + 2)
                    last = nc.scalar.activation(xn[:, b, :], xs[:, b, :], ACT.Square, accum_out=stat[:, b:b + 1])
                last.then_inc(squares_ready, 1)
                act.wait_ge(variance_ready, i + 1)
                nc.scalar.activation(stat[:, 4:6], stat[:, 2:4], ACT.Sqrt).then_inc(root_ready, 1)
                if i < 4:
                    act.wait_ge(rstd_ready, i + 1)
                    copy(xn[:, 0, :], xs[:, 0, :], stat[:, 12:13]).then_inc(xn0_ready, 1)

            def turned_hi(i, gain):
                for k in range(DC):
                    act.wait_ge(h_turned, DC * i + k + 1)
                    copy(h_hi[:, k, :], bank[k][:, 0:T],
                         vec[:, gain + k:gain + k + 1]).then_inc(h_hi_ready, 1)

            def mixer(layer):
                u0 = mixer_base(layer)

                def evac(u, dst, src):
                    act.wait_ge(unit_used, u0 + u + 1)
                    copy(dst, src).then_inc(act_evac, 1)

                def exps(b):
                    keys = P * (b + 1)
                    act.wait_ge(neg_max_ready, TB * layer + b + 1)
                    for h in range(HEADS):
                        nc.scalar.activation(probs[:, h, 0:keys], probs[:, h, 0:keys], ACT.Exp,
                                             bias=stat[:, 24 + h:25 + h], accum_out=stat[:, 32 + h:33 + h])
                    nc.scalar.activation(stat[:, 48:56], stat[:, 40:48], ACT.Exp).then_inc(exps_ready, 1)

                def turned_probs(part):
                    act.wait_ge(probs_turned, 3 * layer + part + 1)
                    if part == 1:
                        act.wait_ge(att_done, TB * layer + 1)
                    if part == 2:
                        act.wait_ge(att_half_done, layer + 1)
                    for q in range(2):
                        last = copy(probs_t[:, q * 512:(q + 1) * 512], bank[5 + q][:, :])
                    last.then_inc(probs_t_ready, 1)

                def attention_hi(b):
                    act.wait_ge(att_done, TB * layer + b + 1)
                    copy(pair_hi[0][:, :].rearrange("p (j t) -> p j t", j=4)[:, :, b * P:(b + 1) * P],
                         bank[4][:, :].rearrange("p (j t) -> p j t", j=4)).then_inc(att_hi_ready, 1)

                def branch_hi(turn, src):
                    if turn == 3:
                        act.wait_ge(pool_scaled, layer + 1)
                    else:
                        act.wait_ge(dve_evac, DVE_EVACS * layer + (4 if turn == 1 else 6))
                    if turn >= 2:
                        act.wait_ge(unit_used, u0 + PROJ_UNITS + 6 * (turn - 1))
                    copy(pair_hi[turn % 2][:, :], src).then_inc(branch_hi_ready, 1)

                norm(2 * layer)
                if layer == 0:
                    split_hi(act, 0)
                turned_hi(2 * layer, V_MIX_G + DC * layer)
                if layer == 0:
                    for s in range(1, AHEAD):
                        split_hi(act, s)
                ahead(u0 + 0)
                ahead(u0 + 1)
                evac(0, qkv_s[:, 0:512], bank[0][:, :])
                ahead(u0 + 2)
                evac(1, qkv_s[:, 512:1024], bank[1][:, :])
                ahead(u0 + 3)
                evac(2, qkv_s[:, 1024:1536], bank[2][:, :])
                ahead(u0 + 4)
                act.wait_ge(v_turned, layer + 1)
                copy(v_nat, bank[3][:, 0:T].rearrange("p (b d) -> p b d", b=TB)).then_inc(v_ready, 1)
                evac(3, t1[:, 0:512], bank[0][:, :])
                ahead(u0 + 5)
                evac(4, t1[:, 512:1024], bank[1][:, :])
                exps(0)
                ahead(u0 + 6)
                ahead(u0 + 7)
                turned_probs(0)
                ahead(u0 + 8)
                attention_hi(0)
                ahead(u0 + 9)
                exps(1)
                branch_hi(1, t1)
                ahead(u0 + 10)
                ahead(u0 + 11)
                act.wait_ge(unit_used, u0 + 11)
                for b in range(TB):
                    last = copy(t3[:, b * 512:(b + 1) * 512], bank[b][:, :])
                last.then_inc(act_evac, 1)
                turned_probs(1)
                ahead(u0 + 12)
                ahead(u0 + 13)
                turned_probs(2)
                ahead(u0 + 14)
                act.wait_ge(dve_evac, DVE_EVACS * (layer + 1))
                evac(13, t1[:, 0:512], bank[1][:, :])
                evac(14, t1[:, 512:1024], bank[2][:, :])
                attention_hi(1)
                for turn in range(BRANCHES):
                    for half in range(2):
                        u = PROJ_UNITS + 6 * turn + 3 * half
                        for q in range(2):
                            ahead(u0 + u + q)
                            act.wait_ge(unit_used, u0 + u + q + 1)
                            n = 16 * layer + 4 * turn + 2 * half + q
                            if n >= 2:
                                act.wait_ge(gate_used, n - 1)
                            nc.scalar.activation(gate_buf[:, q, :], bank[2 * half + q][:, :],
                                                 ACT.Sigmoid).then_inc(act_evac, 1)
                        if turn == BRANCHES - 1 and half == 1:
                            act.wait_ge(gate_used, 16 * layer + 14)
                            copy(h_hi_flat[:, 0:1024], merged_flat[:, 0:1024]).then_inc(merged_hi_ready, 1)
                        ahead(u0 + u + 2)
                        if turn == 1 and half == 0:
                            branch_hi(2, t3)
                        if turn == 2 and half == 0:
                            branch_hi(3, t2)
                act.wait_ge(gate_used, 16 * layer + 16)
                copy(h_hi_flat[:, 1024:2048], merged_flat[:, 1024:2048]).then_inc(merged_hi_ready, 1)
                for u in range(MIX_UNITS - OUT_UNITS, MIX_UNITS):
                    if u0 + u + AHEAD < UNITS1:
                        ahead(u0 + u)

            def dense():
                base = MIX_UNITS
                norm(1)
                turned_hi(1, V_FFN_G)
                ahead(base)
                ahead(base + 1)
                act.wait_ge(unit_used, base + 1)
                nc.scalar.activation(gate_buf[:, 0, :], bank[0][:, :], ACT.Silu).then_inc(silu_ready, 1)
                with act.Fori(0, (SLABS - 1) // 2) as it:
                    for j in range(2):
                        i = 1 + j
                        s = base + 2 + 3 * j
                        more = (6, it)
                        ahead(s, more)
                        act.wait_ge(act_ready, 2 * it + i)
                        copy(pair_hi[j][:, 0:512], gate_buf[:, j, :]).then_inc(act_hi_ready, 1)
                        ahead(s + 1, more)
                        act.wait_ge(unit_used, 6 * it + (s + 1))
                        nc.scalar.activation(gate_buf[:, i % 2, :], bank[i % 2][:, :],
                                             ACT.Silu).then_inc(silu_ready, 1)
                        ahead(s + 2, more)
                act.wait_ge(act_ready, SLABS)
                copy(pair_hi[0][:, 0:512], gate_buf[:, 0, :]).then_inc(act_hi_ready, 1)
                ahead(base + DENSE_UNITS - 1)

            mixer(0)
            dense()
            mixer(1)

            norm(3)
            for k in range(DC):
                act.wait_ge(h_turned, DC * LAYERS + DC + k + 1)
                if k == DC // 2:
                    act.wait_ge(moe_h_ready, TB)
                dst = gate_flat if k < DC // 2 else gain_row
                copy(dst[:, k % 4 * T:(k % 4 + 1) * T], bank[k][:, 0:T],
                     vec[:, V_FFN_G + DC + k:V_FFN_G + DC + k + 1]).then_inc(r_copied, 1)
            for b in range(TB):
                act.wait_ge(moe_h_ready, b + 1)
                copy(h_hi_flat[:, b * D:(b + 1) * D], moe_rows[b]).then_inc(moe_h_hi_ready, 1)
            act.wait_ge(gap_ready, 1)
            nc.scalar.activation(route[:, 88:90], route[:, 86:88], ACT.Exp).then_inc(exp_gap_ready, 1)

            def silu(i, g):
                act.wait_ge(unit_used, EXPERT_UNITS * g + (moe_unit(i, 1) + 1))
                act.wait_ge(h_turned, TURNS_BEFORE + SLABS * g + i)
                nc.scalar.activation(gate_flat[:, 0:256], slab_bank(i)[:, 0:256], ACT.Silu).then_inc(silu_ready, 1)

            def slots_hi(g, used):
                act.wait_ge(unit_used, used)
                for q in range(2):
                    act.wait_ge(gathered, 2 * g + q + 1)
                    copy(pair_hi[0][:, q * 512:(q + 1) * 512], bank[5 + q][:, :]).then_inc(slots_hi_ready, 1)

            def weigh_y(g, used):
                act.wait_ge(unit_used, used)
                act.wait_ge(share_ready, g + 1)
                act.wait_ge(x_updated, X_BEFORE + 4 * g)
                for q in range(2):
                    copy(merged_flat[:, q * 512:(q + 1) * 512], bank[3 + q][:, :], stat[:, 60:61]).then_inc(y_weighted, 1)

            def y_hi(g):
                for q in range(2):
                    cols = slice(q * 512, (q + 1) * 512)
                    act.wait_ge(y_weighted, 2 * g + q + 1)
                    copy(pair_hi[1][:, cols], merged_flat[:, cols]).then_inc(y_hi_ready, 1)

            def step(i, g, y=None, last_turn=False):
                more = (EXPERT_UNITS, g)
                ahead(moe_unit(i, 0), more, last_turn)
                if y is not None and i == 1:
                    weigh_y(y, EXPERT_UNITS * g + moe_unit(1, 0))
                ahead(moe_unit(i, 1), more, last_turn)
                act.wait_ge(h_turned, TURNS_BEFORE + SLABS * g + i)
                copy(act_hi[:, :], bank[2][:, 0:256]).then_inc(act_hi_ready, 1)
                ahead(moe_unit(i, 2), more, last_turn)
                if i == 10 and not last_turn:
                    slots_hi(g + 1, EXPERT_UNITS * g + (moe_unit(10, 1) + 1))
                silu(i, g)
                if y is not None and i == 1:
                    y_hi(y)

            act.wait_ge(route_ready, 1)
            n_pass = act.value_load(n_pass_i[0:1, 0:1], min_val=1, max_val=2)
            with act.Fori(0, n_pass) as r:
                g0 = EXPERTS * r
                for s in range(AHEAD):
                    split_hi(act, UNITS1 + s, (EXPERT_UNITS, g0))
                slots_hi(g0, EXPERT_UNITS * g0 + UNITS1)
                ahead(UNITS1, (EXPERT_UNITS, g0))
                ahead(UNITS1 + 1, (EXPERT_UNITS, g0))
                silu(0, g0)
                for i in range(1, 7):
                    step(i, g0)
                with act.Fori(0, EXPERTS - 1) as e:
                    g = EXPERTS * r + e
                    for i in range(7, SLABS + 1):
                        step(i, g)
                    for i in range(1, 7):
                        step(i, g + 1, y=g)
                g7 = EXPERTS * r + (EXPERTS - 1)
                for i in range(7, SLABS):
                    step(i, g7, last_turn=True)
                act.wait_ge(h_turned, TURNS_BEFORE + SLABS * g7 + SLABS)
                copy(act_hi[:, :], bank[2][:, 0:256]).then_inc(act_hi_ready, 1)
                weigh_y(g7, EXPERT_UNITS * g7 + (moe_unit(SLABS, 0) + 1))
                y_hi(g7)
                act.wait_ge(x_updated, X_BEFORE + 4 * g7 + 2)
            norm(4, X_BEFORE + 4 * EXPERTS * n_pass - 4)
            for b in range(TB):
                act.wait_ge(out_scaled, b + 1)
                act.dma_start(out[:, b, :], xn[:, b, :]).then_inc(out_stored, 16)
            act.wait_ge(out_stored, 16 * TB)

        @block.vector
        def _(dve):
            steps = [0]

            def link(ins):
                steps[0] += 1
                ins.then_inc(dve_step, 1)
                dve.wait_ge(dve_step, steps[0])

            def tt(dst, a, b, op):
                return nc.vector.tensor_tensor(dst, a, b, op)

            def ts(dst, a, s1, s2=None, op0=ALU.mult, op1=None):
                if op1 is None:
                    return nc.vector.tensor_scalar(dst, a, s1, None, op0)
                return nc.vector.tensor_scalar(dst, a, s1, s2, op0, op1)

            def stt(dst, a, s, b, op0, op1):
                return nc.vector.scalar_tensor_tensor(out=dst, in0=a, scalar=s, in1=b, op0=op0, op1=op1)

            def low(dst, src, hi):
                return tt(dst, src, hi.bitcast(F32), ALU.subtract)

            def ahead(s, more=0, last_turn=False):
                if not (last_turn and s + AHEAD >= UNITS1 + EXPERT_UNITS):
                    split_lo(dve, s + AHEAD, more)

            def norm(i):
                dve.wait_ge(squares_ready, i + 1)
                ts(stat[:, 2:4], stat[:, 0:2], 1.0 / D, EPS, ALU.mult, ALU.add).then_inc(variance_ready, 1)
                dve.wait_ge(variance_ready, i + 1)
                dve.wait_ge(root_ready, i + 1)
                link(nc.vector.reciprocal(stat[:, 6:8], stat[:, 4:6]))
                link(tt(stat[:, 8:10], stat[:, 6:8], stat[:, 6:8], ALU.mult))
                link(tt(stat[:, 10:12], stat[:, 8:10], stat[:, 2:4], ALU.mult))
                link(ts(stat[:, 10:12], stat[:, 10:12], -0.5, 1.5, ALU.mult, ALU.add))
                tt(stat[:, 12:14], stat[:, 10:12], stat[:, 6:8], ALU.mult).then_inc(rstd_ready, 1)
                dve.wait_ge(rstd_ready, i + 1)
                if i < 4:
                    ts(xn[:, 1, :], xs[:, 1, :], stat[:, 13:14]).then_inc(xn1_ready, 1)

            def turned_lo(i, gain):
                for k in range(DC):
                    dve.wait_ge(h_hi_ready, DC * i + k + 1)
                    stt(h_lo[:, k, :], bank[k][:, 0:T],
                        vec[:, gain + k:gain + k + 1], h_hi[:, k, :].bitcast(F32),
                        ALU.mult, ALU.subtract).then_inc(h_lo_ready, 1)

            def update_x(n, used, first_bank):
                for q in range(4):
                    if q == 0:
                        dve.wait_ge(sum0_done, n + 1)
                    elif q == 2:
                        dve.wait_ge(unit_used, used)
                    part = xs[:, q // 2, (q % 2) * 512:(q % 2) * 512 + 512]
                    tt(part, part, bank[first_bank + q][:, :], ALU.add).then_inc(x_updated, 1)

            def mixer(layer):
                u0 = mixer_base(layer)

                def unit_done(u):
                    dve.wait_ge(unit_used, u0 + u + 1)

                def scores(b):
                    keys = P * (b + 1)
                    per = 512 // keys
                    dve.wait_ge(scores_done, TB * layer + b + 1)
                    m = mask[:, 256 - keys:256].unsqueeze(1).to_broadcast([P, per, keys])
                    for q in range(HEADS // per):
                        last = stt(probs[:, q * per:(q + 1) * per, 0:keys],
                                   bank[4 + q][:, :].rearrange("p (h k) -> p h k", h=per), HD ** -0.5, m,
                                   ALU.mult, ALU.add)
                    link(last)
                    link(nc.vector.tensor_reduce(stat[:, 16:24], probs[:, :, 0:keys], AX.X, ALU.max))
                    sink = vec[:, V_SINK + HEADS * layer:V_SINK + HEADS * layer + HEADS]
                    link(tt(stat[:, 16:24], stat[:, 16:24], sink, ALU.max))
                    ts(stat[:, 24:32], stat[:, 16:24], -1.0)
                    tt(stat[:, 40:48], sink, stat[:, 16:24], ALU.subtract).then_inc(neg_max_ready, 1)

                def normalise(b):
                    keys = P * (b + 1)
                    dve.wait_ge(exps_ready, TB * layer + b + 1)
                    link(tt(stat[:, 56:64], stat[:, 32:40], stat[:, 48:56], ALU.add))
                    link(nc.vector.reciprocal(stat[:, 64:72], stat[:, 56:64]))
                    r = stat[:, 64:72].unsqueeze(2).to_broadcast([P, HEADS, keys])
                    tt(probs[:, :, 0:keys], probs[:, :, 0:keys], r, ALU.mult).then_inc(probs_ready, 1)

                def attention_lo(b):
                    dve.wait_ge(att_hi_ready, TB * layer + b + 1)

                    def block_of(a):
                        return a.rearrange("p (j t) -> p j t", j=4)[:, :, b * P:(b + 1) * P]

                    low(block_of(pair_lo[0][:, :]), bank[4][:, :].rearrange("p (j t) -> p j t", j=4),
                        block_of(pair_hi[0][:, :])).then_inc(att_lo_ready, 1)

                def branch_lo(turn, src):
                    dve.wait_ge(branch_hi_ready, 3 * layer + turn)
                    low(pair_lo[turn % 2][:, :], src, pair_hi[turn % 2][:, :]).then_inc(branch_lo_ready, 1)

                def conv():
                    z = t1.rearrange("p (c t) -> p c t", c=CT)
                    y = t2.rearrange("p (c t) -> p c t", c=CT)
                    for back in range(3):
                        for c in range(CT):
                            tap = V_CONV + 12 * layer + (2 - back) * CT + c
                            w = vec[:, tap:tap + 1]
                            if back == 0:
                                last = ts(y[:, c, :], z[:, c, :], w)
                            else:
                                last = stt(y[:, c, back:T], z[:, c, 0:T - back], w, y[:, c, back:T],
                                           ALU.mult, ALU.add)
                        link(last)

                def pool():
                    p = t1.rearrange("p (g t) -> p g t", g=CT)
                    dve.wait_ge(act_evac, ACT_EVACS * layer + 8)
                    src = p
                    for g in range(CT):
                        w = 1 << g
                        dst = pool_b if g % 2 else pool_a
                        nc.vector.tensor_copy(dst[:, g:CT, 0:w], src[:, g:CT, 0:w])
                        link(tt(dst[:, g:CT, w:T], src[:, g:CT, w:T], src[:, g:CT, 0:T - w], ALU.add))
                        src = dst
                    for g in range(CT):
                        acc = pool_b if g % 2 else pool_a
                        fix = vec[:, V_FIX + 16 * g:V_FIX + 16 * g + 16]
                        last = tt(acc[:, g, 0:16], acc[:, g, 0:16], fix, ALU.mult)
                    link(last)
                    for g in range(CT):
                        acc = pool_b if g % 2 else pool_a
                        last = stt(p[:, g, :], acc[:, g, :], 1.0 / (2 << g), p[:, g, :], ALU.mult, ALU.subtract)
                    last.then_inc(pooled_ready, 1)

                norm(2 * layer)
                if layer == 0:
                    split_lo(dve, 0)
                turned_lo(2 * layer, V_MIX_G + DC * layer)
                if layer == 0:
                    for s in range(1, AHEAD):
                        split_lo(dve, s)
                for u in range(5):
                    ahead(u0 + u)
                scores(0)
                ahead(u0 + 5)
                unit_done(5)
                dve.wait_ge(act_evac, ACT_EVACS * layer + 5)
                tt(t1[:, 0:512], t1[:, 0:512], bank[2][:, :], ALU.mult).then_inc(dve_evac, 1)
                normalise(0)
                ahead(u0 + 6)
                unit_done(6)
                tt(t1[:, 512:1024], t1[:, 512:1024], bank[0][:, :], ALU.mult).then_inc(dve_evac, 1)
                dve.wait_ge(dve_evac, DVE_EVACS * layer + 2)
                conv()
                ahead(u0 + 7)
                unit_done(7)
                tt(t1[:, 0:512], t2[:, 0:512], bank[1][:, :], ALU.mult).then_inc(dve_evac, 1)
                attention_lo(0)
                ahead(u0 + 8)
                unit_done(8)
                tt(t1[:, 512:1024], t2[:, 512:1024], bank[2][:, :], ALU.mult).then_inc(dve_evac, 1)
                dve.wait_ge(dve_evac, DVE_EVACS * layer + 4)
                scores(1)
                ahead(u0 + 9)
                normalise(1)
                ahead(u0 + 10)
                branch_lo(1, t1)
                ahead(u0 + 11)
                dve.wait_ge(branch_lo_ready, 3 * layer + 1)
                dve.wait_ge(mixed_done, layer + 1)
                for g in range(4):
                    b7 = bank[7 if g < 2 else 3][:, (g % 2) * T:(g % 2) * T + T].rearrange("p (b t) -> p b t", b=TB)
                    last = tt(t1[:, g * T:(g + 1) * T].rearrange("p (b t) -> p b t", b=TB), b7,
                              sgu_bias[:, g, :].unsqueeze(1).to_broadcast([P, TB, P]), ALU.add)
                last.then_inc(mixed_ready, 1)
                dve.wait_ge(mixed_ready, layer + 1)
                unit_done(11)
                tt(t3[:, 0:512], t1[:, 0:512], bank[2][:, :], ALU.mult).then_inc(dve_evac, 1)
                ahead(u0 + 12)
                unit_done(12)
                tt(t3[:, 512:1024], t1[:, 512:1024], bank[0][:, :], ALU.mult).then_inc(dve_evac, 1)
                ahead(u0 + 13)
                ahead(u0 + 14)
                for turn in range(BRANCHES):
                    for half in range(2):
                        u = PROJ_UNITS + 6 * turn + 3 * half
                        ahead(u0 + u)
                        if turn == 0 and half == 0:
                            attention_lo(1)
                        ahead(u0 + u + 1)
                        if turn == 0 and half == 0:
                            pool()
                        if turn == 1 and half == 0:
                            dve.wait_ge(pool_done, layer + 1)
                            for g in range(CT):
                                col = V_POOL + CT * layer + g
                                last = ts(t2[:, g * T:(g + 1) * T], bank[6 + g // 2][:, (g % 2) * T:(g % 2) * T + T],
                                          vec[:, col:col + 1])
                            last.then_inc(pool_scaled, 1)
                        if turn == BRANCHES - 1 and half == 1:
                            dve.wait_ge(merged_hi_ready, 2 * layer + 1)
                            low(h_lo_flat[:, 0:1024], merged_flat[:, 0:1024],
                                h_hi_flat[:, 0:1024]).then_inc(merged_lo_ready, 1)
                        ahead(u0 + u + 2)
                        if half == 0 and turn in (1, 2):
                            branch_lo(turn + 1, t3 if turn == 1 else t2)
                        unit_done(u + 2)
                        for q in range(2):
                            n = 4 * turn + 2 * half + q
                            dve.wait_ge(act_evac, ACT_EVACS * layer + 9 + n)
                            dst = merged_flat[:, (2 * half + q) * 512:(2 * half + q) * 512 + 512]
                            if turn == 0:
                                tt(dst, bank[4 + q][:, :], gate_buf[:, q, :], ALU.mult).then_inc(gate_used, 1)
                            else:
                                link(tt(gate_buf[:, q, :], bank[4 + q][:, :], gate_buf[:, q, :], ALU.mult))
                                dve.wait_ge(gate_used, 16 * layer + 4 * (turn - 1) + 2 * half + q + 1)
                                tt(dst, dst, gate_buf[:, q, :], ALU.add).then_inc(gate_used, 1)
                dve.wait_ge(merged_hi_ready, 2 * layer + 2)
                low(h_lo_flat[:, 1024:2048], merged_flat[:, 1024:2048],
                    h_hi_flat[:, 1024:2048]).then_inc(merged_lo_ready, 1)
                for u in range(MIX_UNITS - OUT_UNITS, MIX_UNITS):
                    if u0 + u + AHEAD < UNITS1:
                        ahead(u0 + u)
                update_x(2 * layer, u0 + MIX_UNITS, 0)

            def dense():
                base = MIX_UNITS
                norm(1)
                turned_lo(1, V_FFN_G)

                def product(parity, n, used):
                    dve.wait_ge(silu_ready, n)
                    dve.wait_ge(unit_used, used)
                    tt(gate_buf[:, parity, :], gate_buf[:, parity, :], bank[2 + parity][:, :],
                       ALU.mult).then_inc(act_ready, 1)

                def split_product(parity, n):
                    dve.wait_ge(act_hi_ready, n)
                    low(pair_lo[parity][:, 0:512], gate_buf[:, parity, :],
                        pair_hi[parity][:, 0:512]).then_inc(act_lo_ready, 1)

                ahead(base)
                ahead(base + 1)
                product(0, 1, base + 2)
                with dve.Fori(0, (SLABS - 1) // 2) as it:
                    for j in range(2):
                        i = 1 + j
                        s = base + 2 + 3 * j
                        more = (6, it)
                        ahead(s, more)
                        split_product(j, 2 * it + i)
                        ahead(s + 1, more)
                        ahead(s + 2, more)
                        product(i % 2, 2 * it + (i + 1), 6 * it + (s + 2))
                split_product(0, SLABS)
                ahead(base + DENSE_UNITS - 1)
                update_x(1, base + DENSE_UNITS, 4)

            dve.wait_ge(vec_loaded, 16)
            nc.vector.tensor_copy(ident_r[:, :], ident).then_inc(ident_ready, 1)
            mixer(0)
            dense()
            mixer(1)

            norm(3)
            dve.wait_ge(gain_loaded, 16)
            for b in range(TB):
                dve.wait_ge(xn0_ready if b == 0 else xn1_ready, 4)
                tt(moe_rows[b], xn[:, b, :], gain_row, ALU.mult).then_inc(moe_h_ready, 1)
            for b in range(TB):
                dve.wait_ge(moe_h_hi_ready, b + 1)
                low(h_lo_flat[:, b * D:(b + 1) * D], moe_rows[b],
                    h_hi_flat[:, b * D:(b + 1) * D]).then_inc(moe_h_lo_ready, 1)
            dve.wait_ge(tables_loaded, 16)
            dve.wait_ge(logits_done, 1)

            def r(a, n=16):
                return route[:, a:a + n]

            def by_expert(a):
                return a.rearrange("p (b e) -> p b e", b=TB)

            def spread(a):
                return route[:, a:a + TB].unsqueeze(2).to_broadcast([P, TB, EXPERTS])

            rank = rank8.unsqueeze(1).to_broadcast([P, TB, EXPERTS])
            for b in range(TB):
                last = tt(r(EXPERTS * b, EXPERTS), bank[b][:, 0:EXPERTS], vec[:, V_RB:V_RB + EXPERTS], ALU.add)
            link(last)

            def choose(values, top, chosen):
                link(nc.vector.tensor_reduce(r(top, TB), by_expert(r(values)), AX.X, ALU.max))
                link(tt(by_expert(r(16)), by_expert(r(values)), spread(top), ALU.is_equal))
                link(tt(by_expert(r(16)), by_expert(r(16)), rank, ALU.mult))
                link(nc.vector.tensor_reduce(r(82, TB), by_expert(r(16)), AX.X, ALU.max))
                link(tt(by_expert(r(chosen)), by_expert(r(16)), spread(82), ALU.is_equal))

            choose(0, 80, 32)
            link(ts(r(64), r(32), -1.0, 1.0, ALU.mult, ALU.add))
            link(tt(r(64), r(64), r(0), ALU.mult))
            link(stt(r(64), r(32), -3e38, r(64), ALU.mult, ALU.add))
            choose(64, 84, 48)
            link(tt(r(112), r(32), r(48), ALU.add))
            tt(r(86, TB), r(84, TB), r(80, TB), ALU.subtract).then_inc(gap_ready, 1)
            dve.wait_ge(gap_ready, 1)
            dve.wait_ge(exp_gap_ready, 1)
            link(ts(r(90, TB), r(88, TB), 1.0, None, ALU.add))
            link(nc.vector.reciprocal(r(92, TB), r(90, TB)))
            link(tt(r(94, TB), r(88, TB), r(92, TB), ALU.mult))
            link(tt(by_expert(r(96)), by_expert(r(32)), spread(92), ALU.mult))
            link(tt(by_expert(r(16)), by_expert(r(48)), spread(94), ALU.mult))
            link(tt(r(96), r(96), r(16), ALU.add))
            for half in range(2):
                last = nc.vector.tensor_copy(combine_r[:, :, 8 * half:8 * half + 8, 0], by_expert(r(96)))
            link(last)
            for half in range(2):
                last = tt(combine_r[:, :, 8 * half:8 * half + 8, 1], by_expert(r(96)),
                          combine_r[:, :, 0:8, 0].bitcast(F32), ALU.subtract)
            link(last)
            dve.wait_ge(places_done, 1)
            places = r(128, 32).rearrange("p (b g) -> p b g", b=TB)
            link(stt(places[:, :, 0:8], by_expert(bank[6][:, 0:16]), 1.0, by_expert(r(112)), ALU.add, ALU.mult))
            link(ts(places[:, :, 0:8], places[:, :, 0:8], 1.0, None, ALU.subtract))
            link(ts(places[:, :, 8:16], places[:, :, 0:8], float(P), None, ALU.subtract))
            link(nc.vector.tensor_reduce(r(200, 1), bank[6][:, 16:24], AX.X, ALU.max))
            link(ts(r(201, 1), r(200, 1), P + 0.5, 1.0, ALU.is_ge, ALU.add))
            nc.vector.tensor_copy(n_pass_i[:, :], r(201, 1)).then_inc(route_ready, 1)
            dve.wait_ge(route_ready, 1)

            def choose_slots(g, first=False):
                if not first:
                    dve.wait_ge(onehot_turned, g)
                    dve.wait_ge(gathered, 2 * g)
                for b in range(TB):
                    place = route[:, bass.ds(g + (128 + 16 * b), 1)]
                    last = nc.vector.tensor_scalar(onehot[:, b, :], iota, place, None, ALU.is_equal)
                last.then_inc(onehot_ready, 1)

            def slots_lo(g, halves=(0, 1)):
                for q in halves:
                    dve.wait_ge(slots_hi_ready, 2 * g + q + 1)
                    low(pair_lo[0][:, q * 512:(q + 1) * 512], bank[5 + q][:, :],
                        pair_hi[0][:, q * 512:(q + 1) * 512]).then_inc(slots_lo_ready, 1)

            def split_y(g):
                for q in range(2):
                    cols = slice(q * 512, (q + 1) * 512)
                    dve.wait_ge(y_hi_ready, 2 * g + q + 1)
                    low(pair_lo[1][:, cols], merged_flat[:, cols], pair_hi[1][:, cols]).then_inc(y_lo_ready, 1)

            def turned_onehot(g):
                dve.wait_ge(onehot_turned, g + 1)
                nc.vector.tensor_copy(onehot_t[:, :], bank[7][:, 0:T]).then_inc(onehot_t_ready, 1)
                nc.vector.tensor_reduce(stat[:, 60:61], bank[7][:, T:T + 2], AX.X, ALU.add).then_inc(share_ready, 1)

            def add_scattered(g, q, last_turn=False):
                dve.wait_ge(scattered, 4 * g + q + 1)
                dve.wait_ge(x_updated, X_BEFORE + 4 * g)
                part = xs[:, q // 2, (q % 2) * 512:(q % 2) * 512 + 512]
                tt(part, part, scatter_bank(q, last_turn)[:, :], ALU.add).then_inc(x_updated, 1)

            def product(i, g):
                dve.wait_ge(silu_ready, SLABS * (g + 1) + i + 1)
                tt(gate_flat[:, 0:256], gate_flat[:, 0:256], slab_bank(i)[:, 256:512],
                   ALU.mult).then_inc(act_ready, 1)

            def slab_lo(i, g):
                dve.wait_ge(act_hi_ready, SLABS * (g + 1) + i + 1)
                low(act_lo[:, :], bank[2][:, 0:256], act_hi[:, :]).then_inc(act_lo_ready, 1)

            def step(i, g, y=None, last_turn=False):
                more = (EXPERT_UNITS, g)
                ahead(moe_unit(i, 0), more, last_turn)
                slab_lo(i - 1, g)
                ahead(moe_unit(i, 1), more, last_turn)
                if y is not None:
                    if i == 2:
                        split_y(y)
                    elif i > 2:
                        add_scattered(y, i - 3)
                if i == 7:
                    turned_onehot(g)
                    if not last_turn:
                        choose_slots(g + 1)
                if i == 10 and not last_turn:
                    slots_lo(g + 1)
                ahead(moe_unit(i, 2), more, last_turn)
                product(i, g)

            n_pass = dve.value_load(n_pass_i[0:1, 0:1], min_val=1, max_val=2)
            with dve.Fori(0, n_pass) as rr:
                g0 = EXPERTS * rr
                choose_slots(g0, first=True)
                for s in range(AHEAD):
                    split_lo(dve, UNITS1 + s, (EXPERT_UNITS, g0))
                    if s < 2:
                        slots_lo(g0, (s,))
                ahead(UNITS1, (EXPERT_UNITS, g0))
                ahead(UNITS1 + 1, (EXPERT_UNITS, g0))
                product(0, g0)
                for i in range(1, 7):
                    step(i, g0)
                with dve.Fori(0, EXPERTS - 1) as e:
                    g = EXPERTS * rr + e
                    for i in range(7, SLABS + 1):
                        step(i, g)
                    for i in range(1, 7):
                        step(i, g + 1, y=g)
                g7 = EXPERTS * rr + (EXPERTS - 1)
                for i in range(7, SLABS):
                    step(i, g7, last_turn=True)
                slab_lo(SLABS - 1, g7)
                split_y(g7)
                for q in range(4):
                    add_scattered(g7, q, last_turn=True)
                dve.wait_ge(x_updated, X_BEFORE + 4 * g7 + 4)
            norm(4)
            dve.wait_ge(final_gain_loaded, 16)
            for b in range(TB):
                stt(xn[:, b, :], xs[:, b, :], stat[:, 12 + b:13 + b], gain_row, ALU.mult,
                    ALU.mult).then_inc(out_scaled, 1)

        @block.tensor
        def _(pe):
            def mm(dst, lhs_t, rhs, start, stop):
                return nc.tensor.matmul(dst, lhs_t, rhs, start=start, stop=stop)

            def mm3(dst, a, b, start, stop):
                mm(dst, a[0], b[0], start, False)
                mm(dst, a[0], b[1], False, False)
                return mm(dst, a[1], b[0], False, stop)

            def weights(s, more, cols):
                half, start = cols.start // HALF, cols.start % HALF
                start += hi_half(s, half)
                return w_hi[:, start:start + cols.stop - cols.start], lo_of(s)[:, cols]

            def await_split(s, more=0):
                pe.wait_ge(hi_ready, at(s + 1, more))
                pe.wait_ge(lo_ready, at(s + 1, more))

            def h_part(k, lo=0, n=T):
                return h_hi[:, k, lo:lo + n], h_lo[:, k, lo:lo + n]

            def pair_part(i, lo, n):
                return pair_hi[i][:, lo:lo + n], pair_lo[i][:, lo:lo + n]

            def turn_rows(i):
                pe.wait_ge(vec_loaded, 16)
                pe.wait_ge(xn0_ready, i + 1)
                pe.wait_ge(xn1_ready, i + 1)
                for k in range(DC):
                    for b in range(TB):
                        last = nc.tensor.transpose(bank[k][:, b * P:(b + 1) * P], xn[:, b, k * P:(k + 1) * P], ident)
                    last.then_inc(h_turned, 1)

            def project(s, dst, tiles=2, norm_no=None, more=0):
                await_split(s, more)
                for t in range(tiles):
                    for k in range(DC):
                        if norm_no is not None and t == 0:
                            pe.wait_ge(h_lo_ready, DC * norm_no + k + 1)
                        last = mm3(dst[:, t * T:(t + 1) * T], weights(s, more, slice(k * T + t * P, k * T + (t + 1) * P)),
                                   h_part(k), k == 0, k == DC - 1)
                return last.then_inc(unit_used, 1)

            def mixer(layer):
                u0 = mixer_base(layer)

                def acts(n):
                    pe.wait_ge(act_evac, ACT_EVACS * layer + n)

                def dves(n):
                    pe.wait_ge(dve_evac, DVE_EVACS * layer + n)

                def scores(b):
                    keys = P * (b + 1)
                    per = 512 // keys
                    for h in range(HEADS):
                        half = slice(HD * (h // 4), HD * (h // 4) + HD)
                        last = mm(bank[4 + h // per][:, (h % per) * keys:(h % per + 1) * keys],
                                  q_t[half, h % 4, b * P:(b + 1) * P], k_t[half, 0:keys], True, True)
                    last.then_inc(scores_done, 1)

                def turn_probs(part):
                    pe.wait_ge(probs_ready, TB * layer + (2 if part else 1))
                    if 3 * layer + part:
                        pe.wait_ge(probs_t_ready, 3 * layer + part)
                    for n in range(8):
                        h, kb = (n, 0) if part == 0 else (4 * (part - 1) + n // 2, n % 2)
                        last = nc.tensor.transpose(bank[5 + n // 4][:, (n % 4) * P:(n % 4 + 1) * P],
                                                   probs[:, h, kb * P:(kb + 1) * P], ident)
                    last.then_inc(probs_turned, 1)

                def values(part):
                    pe.wait_ge(probs_t_ready, 3 * layer + part + 1)
                    blocks = 1 if part == 0 else 2
                    for h in range(HEADS) if part == 0 else range(4 * (part - 1), 4 * part):
                        half = slice(HD * (h // 4), HD * (h // 4) + HD)
                        for kb in range(blocks):
                            n = (h if part == 0 else (h % 4) * 2 + kb) * P
                            last = mm(bank[4][half, (h % 4) * P:(h % 4 + 1) * P], v_nat[:, kb, half],
                                      probs_t[:, n:n + P], kb == 0, kb == blocks - 1)
                    last.then_inc(att_half_done if part == 1 else att_done, 1)

                turn_rows(2 * layer)
                project(u0 + 0, bank[0][:, :], norm_no=2 * layer)
                project(u0 + 1, bank[1][:, :])
                project(u0 + 2, bank[2][:, :])
                acts(1)
                project(u0 + 3, bank[0][:, :])
                acts(3)
                for b in range(TB):
                    last = nc.tensor.transpose(bank[3][:, b * P:(b + 1) * P], v_t[:, b * P:(b + 1) * P], ident)
                last.then_inc(v_turned, 1)
                scores(0)
                project(u0 + 4, bank[1][:, :])
                project(u0 + 5, bank[2][:, :])
                acts(4)
                project(u0 + 6, bank[0][:, :])
                turn_probs(0)
                acts(5)
                project(u0 + 7, bank[1][:, :])
                pe.wait_ge(v_ready, layer + 1)
                values(0)
                dves(1)
                project(u0 + 8, bank[2][:, :])
                pe.wait_ge(att_lo_ready, TB * layer + 1)
                scores(1)
                for j in range(2):
                    await_split(u0 + 9 + j)
                    if j == 0:
                        dves(3)
                    for b in range(TB):
                        for kk in range(4):
                            k = 4 * j + kk
                            last = mm3(bank[b][:, :], h_part(k, b * P, P),
                                       weights(u0 + 9 + j, 0, slice(kk * 512, kk * 512 + 512)), k == 0, k == DC - 1)
                    last.then_inc(unit_used, 1)
                dves(4)
                project(u0 + 11, bank[2][:, :])
                turn_probs(1)
                acts(6)
                pe.wait_ge(sgu_masked, layer + 1)
                for g in range(4):
                    for b in range(TB):
                        last = mm(bank[7 if g < 2 else 3][:, (g % 2) * T + b * P:(g % 2) * T + (b + 1) * P],
                                  t3[:, b * 512 + g * P:b * 512 + (g + 1) * P], sgu_wt[:, g, :], True, True)
                last.then_inc(mixed_done, 1)
                project(u0 + 12, bank[0][:, :])
                values(1)
                turn_probs(2)
                project(u0 + 13, bank[1][:, :])
                dves(5)
                project(u0 + 14, bank[2][:, :])
                values(2)
                for turn in range(BRANCHES):
                    for half in range(2):
                        u = PROJ_UNITS + 6 * turn + 3 * half
                        for q in range(2):
                            if turn:
                                acts(9 + 4 * (turn - 1) + 2 * half + q)
                            elif half == 0:
                                dves(6) if q == 0 else acts(7)
                            else:
                                acts(8) if q == 0 else pe.wait_ge(mixed_ready, layer + 1)
                            project(u0 + u + q, bank[2 * half + q][:, :])
                        await_split(u0 + u + 2)
                        if turn == 0:
                            pe.wait_ge(att_lo_ready, TB * (layer + 1))
                        else:
                            pe.wait_ge(branch_lo_ready, 3 * layer + turn)
                        if turn or half:
                            pe.wait_ge(gate_used, 16 * layer + 4 * turn + 2 * half)
                        for t in range(4):
                            for c in range(CT):
                                last = mm3(bank[4 + t // 2][:, (t % 2) * T:(t % 2) * T + T],
                                           weights(u0 + u + 2, 0, slice(c * 512 + t * P, c * 512 + (t + 1) * P)),
                                           pair_part(turn % 2, c * T, T), c == 0, c == CT - 1)
                        last.then_inc(unit_used, 1)
                        if turn == 0 and half == 1:
                            pe.wait_ge(pooled_ready, layer + 1)
                            for g in range(CT):
                                last = mm(bank[6 + g // 2][:, (g % 2) * T:(g % 2) * T + T], pool_w[:, g, :],
                                          t1[:, g * T:(g + 1) * T], True, True)
                            last.then_inc(pool_done, 1)
                for j in range(OUT_UNITS):
                    s = u0 + MIX_UNITS - OUT_UNITS + j
                    await_split(s)
                    pe.wait_ge(merged_lo_ready, 2 * layer + 1 + j // 2)
                    if j == 0:
                        acts(ACT_EVACS)
                    for b in range(TB):
                        for kk in range(2):
                            k = 2 * j + kk
                            for half in range(2):
                                cols = slice(kk * D + half * 512, kk * D + half * 512 + 512)
                                last = mm3(bank[2 * b + half][:, :], h_part(k, b * P, P),
                                           weights(s, 0, cols), k == 0, k == DC - 1)
                        if b == 0 and j == OUT_UNITS - 1:
                            last.then_inc(sum0_done, 1)
                    last.then_inc(unit_used, 1)

            def dense():
                base = MIX_UNITS

                def down(s, parity, n, first=False, more=0, complete=False):
                    await_split(s, more)
                    pe.wait_ge(act_lo_ready, n)
                    for b in range(TB):
                        for f in range(2):
                            for half in range(2):
                                cols = slice(f * D + half * 512, f * D + half * 512 + 512)
                                last = mm3(bank[4 + 2 * b + half][:, :], pair_part(parity, f * T + b * P, P),
                                           weights(s, more, cols), first and f == 0, complete and f == 1)
                        if b == 0 and complete:
                            last.then_inc(sum0_done, 1)
                    last.then_inc(unit_used, 1)

                turn_rows(1)
                project(base, bank[0][:, :], norm_no=1)
                project(base + 1, bank[2][:, :])
                project(base + 2, bank[1][:, :])
                project(base + 3, bank[3][:, :])
                down(base + 4, 0, 1, True)
                pe.wait_ge(act_ready, 1)
                project(base + 5, bank[0][:, :])
                project(base + 6, bank[2][:, :])
                down(base + 7, 1, 2, False)
                with pe.Fori(1, (SLABS - 1) // 2) as it:
                    for j in range(2):
                        i = 1 + j
                        s = base + 2 + 3 * j
                        more = (6, it)
                        pe.wait_ge(act_ready, 2 * it + (i - 1))
                        project(s, bank[i % 2][:, :], more=more)
                        project(s + 1, bank[2 + i % 2][:, :], more=more)
                        down(s + 2, j, 2 * it + i, False, more)
                down(base + DENSE_UNITS - 1, 0, SLABS, False, complete=True)

            def router():
                turn_rows(3)
                for k in range(DC):
                    pe.wait_ge(r_copied, max(k + 1, TB))
                    rows = gate_flat if k < DC // 2 else gain_row
                    for b in range(TB):
                        at_row = k % 4 * T + b * P
                        last = mm(bank[b][:, 0:EXPERTS], rows[:, at_row:at_row + P],
                                  vec[:, V_RW + EXPERTS * k:V_RW + EXPERTS * (k + 1)], k == 0, k == DC - 1)
                last.then_inc(logits_done, 1)
                pe.wait_ge(tables_loaded, 16)
                pe.wait_ge(gap_ready, 1)
                chosen = [route[:, 112 + EXPERTS * b:112 + EXPERTS * (b + 1)] for b in range(TB)]
                mm(bank[6][:, 0:8], earlier, chosen[0], True, True)
                mm(bank[6][:, 8:16], ones, chosen[0], True, False)
                mm(bank[6][:, 8:16], earlier, chosen[1], False, True)
                mm(bank[6][:, 16:24], ones, chosen[0], True, False)
                mm(bank[6][:, 16:24], ones, chosen[1], False, True).then_inc(places_done, 1)

            def gather(g, first=False):
                pe.wait_ge(onehot_ready, g + 1)
                if not first:
                    pe.wait_ge(slots_lo_ready, 2 * g)
                pe.wait_ge(moe_h_lo_ready, TB)
                for k in range(DC):
                    dst = bank[5 + k // 4][:, (k % 4) * P:(k % 4 + 1) * P]
                    for b in range(TB):
                        rows = slice(b * D + k * P, b * D + (k + 1) * P)
                        mm(dst, h_hi_flat[:, rows], onehot[:, b, :], b == 0, False)
                        last = mm(dst, h_lo_flat[:, rows], onehot[:, b, :], False, b == TB - 1)
                    if k % 4 == 3:
                        last.then_inc(gathered, 1)

            def turn_onehot(g):
                pe.wait_ge(x_updated, X_BEFORE + 4 * g)
                pe.wait_ge(ident_ready, 1)
                for b in range(TB):
                    mm(bank[7][:, b * P:(b + 1) * P], onehot[:, b, :], ident_r[:, :], True, True)
                for b in range(TB):
                    share = combine_r[:, b, bass.ds(g, 1), :].rearrange("p g c -> p (g c)")
                    last = mm(bank[7][:, T:T + 2], onehot[:, b, :], share, b == 0, b == TB - 1)
                last.then_inc(onehot_turned, 1)

            def scatter(g, q, last_turn=False):
                pe.wait_ge(y_lo_ready, 2 * g + q % 2 + 1)
                pe.wait_ge(onehot_t_ready, g + 1)
                if not last_turn:
                    pe.wait_ge(x_updated, X_BEFORE + 4 * g + q)
                dst = scatter_bank(q, last_turn)[:, :]
                tokens = onehot_t[:, (q // 2) * P:(q // 2 + 1) * P]
                cols = slice((q % 2) * 512, (q % 2) * 512 + 512)
                mm(dst, tokens, pair_hi[1][:, cols], True, False)
                mm(dst, tokens, pair_lo[1][:, cols], False, True).then_inc(scattered, 1)

            def gate_up(i, j, g):
                s = moe_unit(i, j)
                if i % SLABS == 0:
                    turn = g + i // SLABS
                    pe.wait_ge(slots_hi_ready, 2 * turn + j + 1)
                    pe.wait_ge(slots_lo_ready, 2 * turn + j + 1)
                await_split(s, (EXPERT_UNITS, g))
                for kk in range(4):
                    k = 4 * j + kk
                    last = mm3(slab_bank(i)[:, :], pair_part(0, k * P, P),
                               weights(s, 0, slice(kk * 512, kk * 512 + 512)), k == 0, k == DC - 1)
                last.then_inc(unit_used, 1)

            def turn_slab(i, g):
                pe.wait_ge(act_ready, SLABS * (g + 1) + i + 1)
                pe.wait_ge(act_lo_ready, SLABS * (g + 1) + i)
                for f in range(2):
                    last = nc.tensor.transpose(bank[2][:, f * P:(f + 1) * P], gate_flat[:, f * P:(f + 1) * P], ident)
                last.then_inc(h_turned, 1)

            def down_slab(i, g, y=None, last_turn=False):
                s = moe_unit(i + 1, 0 if last_turn and i == SLABS - 1 else 2)
                await_split(s, (EXPERT_UNITS, g))
                pe.wait_ge(act_lo_ready, SLABS * (g + 1) + i + 1)
                if i == 0 and y is not None:
                    pe.wait_ge(y_weighted, 2 * y + 2)
                for f in range(2):
                    for half in range(2):
                        cols = slice(f * D + half * 512, f * D + half * 512 + 512)
                        last = mm3(bank[3 + half][:, :], (act_hi[:, f * P:(f + 1) * P], act_lo[:, f * P:(f + 1) * P]),
                                   weights(s, 0, cols), i == 0 and f == 0, i == SLABS - 1 and f == 1)
                last.then_inc(unit_used, 1)

            def step(i, g, y=None, last_turn=False):
                pe.wait_ge(act_ready, SLABS * (g + 1) + (i - 1))
                gate_up(i, 0, g)
                turn_slab(i - 1, g)
                gate_up(i, 1, g)
                down_slab(i - 1, g, y)
                if y is not None and 2 <= i < 6:
                    scatter(y, i - 2)
                if i == 6:
                    turn_onehot(g)
                if i == 7 and not last_turn:
                    gather(g + 1)

            mixer(0)
            dense()
            mixer(1)
            router()
            pe.wait_ge(route_ready, 1)
            n_pass = pe.value_load(n_pass_i[0:1, 0:1], min_val=1, max_val=2)
            with pe.Fori(0, n_pass) as r:
                g0 = EXPERTS * r
                gather(g0, first=True)
                gate_up(0, 0, g0)
                gate_up(0, 1, g0)
                for i in range(1, 7):
                    step(i, g0)
                with pe.Fori(0, EXPERTS - 1) as e:
                    g = EXPERTS * r + e
                    for i in range(7, SLABS + 1):
                        step(i, g)
                    for i in range(1, 7):
                        step(i, g + 1, y=g)
                g7 = EXPERTS * r + (EXPERTS - 1)
                for i in range(7, SLABS):
                    step(i, g7, last_turn=True)
                turn_slab(SLABS - 1, g7)
                down_slab(SLABS - 1, g7, last_turn=True)
                for q in range(4):
                    scatter(g7, q, last_turn=True)
                pe.wait_ge(x_updated, X_BEFORE + 4 * g7 + 4)



def kernel(**inputs):
    import numpy as np
    import concourse.bacc as bacc
    from concourse.bass_utils import run_bass_kernel_spmd

    a = {k: np.asarray(v) for k, v in inputs.items()}

    def still(w):
        return w.reshape(DC, P, 256).transpose(1, 0, 2).reshape(1, P, UNIT)

    def moving(w, cols):
        n = UNIT // cols
        return w.reshape(-1, n, P, cols).transpose(0, 2, 1, 3).reshape(-1, P, UNIT)

    paired = np.concatenate([np.r_[HD * j:HD * j + HD, 256 + HD * j:256 + HD * j + HD] for j in range(4)])

    def mixer_units(layer):
        w = a["w_in"][layer]
        out = [still(w[:, paired[0:256]]), still(w[:, paired[256:512]]), still(w[:, 512:768])]

        def two(start):
            return [still(w[:, start:start + 256]), still(w[:, start + 256:start + 512])]

        cb, cc, cx, p, u, sv, gates = 768, 1280, 1792, 2304, 2816, 3328, 3840
        out += two(cc) + two(cx) + two(cb) + [moving(w[:, sv:sv + 512], 512)] + two(u) + two(p)
        for branch in BRANCH_ORDER:
            wb = a["w_branch"][layer, branch]
            if branch == 0:
                wb = wb[paired]
            for half in range(2):
                out += two(gates + branch * D + half * 512)
                out.append(moving(wb[:, half * 512:half * 512 + 512], 512))
        out.append(moving(a["w_out"][layer], D))
        return out

    def dense_units():
        gate, up, down = (a[f"dense_w_{n}"][0] for n in ("gate", "up", "down"))
        downs = moving(down, D)
        out = []
        for i in range(SLABS):
            out += [still(gate[:, 256 * i:256 * i + 256]), still(up[:, 256 * i:256 * i + 256])]
            if i:
                out.append(downs[i - 1:i])
        return out + [downs[SLABS - 1:]]

    def moe_units():
        gate, up, down = (a[f"moe_w_{n}"][0] for n in ("gate", "up", "down"))
        s = np.empty((MOE_UNITS, P, UNIT), gate.dtype)
        at_unit = 0
        late = None
        for e in range(EXPERTS):
            downs = moving(down[e], D)
            for i in range(SLABS):
                cols = slice(256 * i, 256 * i + 256)
                s[at_unit:at_unit + 2] = moving(np.concatenate([gate[e][:, cols], up[e][:, cols]], 1), 512)
                at_unit += 2
                if late is not None:
                    s[at_unit] = late
                    at_unit += 1
                late = downs[i]
        s[at_unit] = late
        return s

    def spread(v):
        return np.broadcast_to(v.reshape(1, -1), (P, v.size))

    def by_chunk(v):
        return v.reshape(-1, P).T

    t = np.arange(P)
    keys = np.arange(2 * P)
    rel = t[:, None] + P - keys[None, :]
    mask = np.where((rel >= 0) & (rel < P), 0.0, NEG).astype(np.float32)
    fix = np.stack([(2 << g) / np.minimum(np.arange(16) + 1, 2 << g) for g in range(CT)]).astype(np.float32)
    small = np.concatenate([
        by_chunk(a["ln_mix_g"]), by_chunk(a["ln_ffn_g"]), by_chunk(a["conv_w"]), by_chunk(a["pool_scale"]),
        spread(a["attn_sinks"]), spread(a["router_b"][0]),
        a["router_w"][0].reshape(DC, P, EXPERTS).transpose(1, 0, 2).reshape(P, DC * EXPERTS),
        spread(fix), mask, np.eye(P, dtype=np.float32)], 1)
    tables = np.concatenate([
        spread(np.arange(P, dtype=np.float32)), np.triu(np.ones((P, P), np.float32), 1),
        np.ones((P, P), np.float32), spread(8 - np.arange(8, dtype=np.float32)), np.zeros((P, 120), np.float32)], 1)
    layer_weights = np.stack([np.concatenate([
        a["sgu_w"][n].transpose(2, 0, 1).reshape(P, 512), a["pool_w"][n].transpose(1, 0, 2).reshape(P, 512),
        spread(a["sgu_b"][n])], 1) for n in range(LAYERS)])
    gains = np.stack([spread(a["ln_ffn_g"][1]), spread(a["ln_final_g"])])
    arrays = {
        "x": a["x"].reshape(TB, P, D).transpose(1, 0, 2),
        "small": small,
        "tables": tables,
        "layer_weights": layer_weights,
        "gains": gains,
        "stream1": np.concatenate(mixer_units(0) + dense_units() + mixer_units(1)),
        "stream2": moe_units(),
    }
    arrays = {k: np.ascontiguousarray(v) for k, v in arrays.items()}
    nc = bacc.Bacc("TRN2", target_bir_lowering=False, num_devices=1)
    args = [nc.dram_tensor(n, v.shape, F32, kind="ExternalInput").ap() for n, v in arrays.items()]
    out = nc.dram_tensor("out", (T, D), F32, kind="ExternalOutput").ap()
    trunk(nc, *args, out.rearrange("(b p) d -> p b d", p=P))
    r = run_bass_kernel_spmd(nc, [arrays], core_ids=[0])
    return r.results[0]["out"].reshape(1, T, D)
```
